# Optimizing a Trainium2 kernel written in Bass

```python
import math
import jax
import jax.numpy as jnp
from jax import lax
import numpy as np

D_MODEL = 1024
BATCH = 1
SEQ = 512
DEPTH = 1
DEC_BATCH = 8
DEC_SEQ = 1
PAST_LEN = 2048
PAGE_SIZE = 128

N_META = 16
M_HEADS = 4
M_DK = D_MODEL // (2 * M_HEADS)
M_DV = D_MODEL // (2 * M_HEADS)
M_WIDTH = M_HEADS * M_DV
M_CHUNK = 64
A_HD = 64
A_HEADS = D_MODEL // (2 * A_HD)
A_KV_HEADS = 2
A_GROUP = A_HEADS // A_KV_HEADS
A_WIDTH = A_HEADS * A_HD
WINDOW = 128
A_BLOCK = 128
MIX_WIDTH = M_WIDTH + A_WIDTH
REL_BUCKETS = 32
REL_MAX_DIST = 128
N_EXPERTS = 32
TOP_K = 4
D_FF = D_MODEL
SWIGLU_LIMIT = 7.0
SWIGLU_ALPHA = 1.702
MOE_BLOCK = 256
DN_ALPHA = (2.0 * DEPTH) ** 0.25
DN_BETA = (8.0 * DEPTH) ** -0.25
LN_EPS = 1e-5
IN_WIDTHS = (M_HEADS * M_DK, M_HEADS * M_DK, M_WIDTH, M_WIDTH, M_HEADS, M_HEADS,
             A_WIDTH, A_KV_HEADS * A_HD, A_KV_HEADS * A_HD)
N_IN = sum(IN_WIDTHS)
F32 = jnp.float32

kernel_name = 'hymba_mlstm_swa_moe_decode_step'

def layer_norm(x, g, b):
    xf = x.astype(F32)
    mu = jnp.mean(xf, -1, keepdims=True)
    var = jnp.mean(jnp.square(xf - mu), -1, keepdims=True)
    return ((xf - mu) * lax.rsqrt(var + LN_EPS) * g.astype(F32) + b.astype(F32)).astype(x.dtype)

def rms_norm(x, g):
    xf = x.astype(F32)
    r = lax.rsqrt(jnp.mean(jnp.square(xf), -1, keepdims=True) + LN_EPS)
    return (xf * r * g.astype(F32)).astype(x.dtype)

def rel_bucket(dist):
    exact = REL_BUCKETS // 2
    d = jnp.maximum(dist, 0)
    log_b = exact + (jnp.log(jnp.maximum(d, 1).astype(F32) / exact)
                     / math.log(REL_MAX_DIST / exact) * (REL_BUCKETS - exact)).astype(jnp.int32)
    return jnp.where(d < exact, d, jnp.minimum(log_b, REL_BUCKETS - 1))

def rel_bias_heads(rel_table, dist):
    b = rel_table.astype(F32)[rel_bucket(dist)]
    return jnp.moveaxis(b, -1, 0).reshape(A_KV_HEADS, A_GROUP, *dist.shape)

def sink_softmax(s, sinks):
    sk = sinks.astype(F32).reshape(A_KV_HEADS, A_GROUP, 1)
    m = jnp.maximum(jnp.max(s, -1), sk)
    p = jnp.exp(s - m[..., None])
    return p / (jnp.sum(p, -1) + jnp.exp(sk - m))[..., None]

def split_projections(x, w_in, b_i, b_f):
    B, L, _ = x.shape
    proj = x @ w_in
    pts = [int(p) for p in np.cumsum(IN_WIDTHS)[:-1]]
    qm, km, vm, om, im, fm, qa, ka, va = jnp.split(proj, pts, axis=-1)
    heads = lambda a, h: a.reshape(B, L, h, -1)
    t = lambda a: jnp.swapaxes(a, 1, 2).astype(F32)
    q_m = t(heads(qm, M_HEADS))
    k_m = t(heads(km, M_HEADS)) * (M_DK ** -0.5)
    v_m = t(heads(vm, M_HEADS))
    ig = t(im + b_i)
    lf = jax.nn.log_sigmoid(t(fm + b_f))
    att_in = (heads(qa, A_HEADS), heads(ka, A_KV_HEADS), heads(va, A_KV_HEADS))
    return (q_m, k_m, v_m, ig, lf), om, att_in

def mlstm_chunk(carry, inp):
    C, n, m = carry
    q, k, v, ig, lf = inp
    L = q.shape[2]
    b = jnp.cumsum(lf, axis=-1)
    causal = jnp.tril(jnp.ones((L, L), bool))
    D = jnp.where(causal, b[..., :, None] - b[..., None, :] + ig[..., None, :], -jnp.inf)
    inter = b + m[..., None]
    m_t = jnp.maximum(inter, jnp.max(D, -1))
    w_inter = jnp.exp(inter - m_t)
    S = jnp.einsum('bhtd,bhsd->bhts', q, k) * jnp.exp(D - m_t[..., None])
    num = w_inter[..., None] * jnp.einsum('bhvd,bhtd->bhtv', C, q) + jnp.einsum('bhts,bhsv->bhtv', S, v)
    den = w_inter * jnp.einsum('bhd,bhtd->bht', n, q) + jnp.sum(S, -1)
    h = num / jnp.maximum(jnp.abs(den), jnp.exp(-m_t))[..., None]
    bL = b[..., -1]
    g = ig + bL[..., None] - b
    m_new = jnp.maximum(bL + m, jnp.max(g, -1))
    a = jnp.exp(bL + m - m_new)
    wg = jnp.exp(g - m_new[..., None])
    C_new = a[..., None, None] * C + jnp.einsum('bhs,bhsv,bhsd->bhvd', wg, v, k)
    n_new = a[..., None] * n + jnp.einsum('bhs,bhsd->bhd', wg, k)
    return (C_new, n_new, m_new), h

def mlstm_prompt(q, k, v, ig, lf):
    B, H, L, _ = q.shape
    init = (jnp.zeros((B, H, M_DV, M_DK), F32), jnp.zeros((B, H, M_DK), F32), jnp.zeros((B, H), F32))
    st, h_meta = mlstm_chunk(init, tuple(a[:, :, :N_META] for a in (q, k, v, ig, lf)))
    nc = (L - N_META) // M_CHUNK

    def to_chunks(a):
        a = a[:, :, N_META:]
        return jnp.moveaxis(a.reshape(B, H, nc, M_CHUNK, *a.shape[3:]), 2, 0)

    st, h_rest = lax.scan(mlstm_chunk, st, tuple(to_chunks(a) for a in (q, k, v, ig, lf)))
    h_rest = jnp.moveaxis(h_rest, 0, 2).reshape(B, H, nc * M_CHUNK, M_DV)
    return jnp.concatenate([h_meta, h_rest], axis=2), st

def swa_prompt(q, k, v, sinks, rel_table):
    B, L = q.shape[:2]
    pad = (-N_META) % A_BLOCK
    nq = (L + pad) // A_BLOCK
    qb = jnp.pad(q.astype(F32), ((0, 0), (pad, 0), (0, 0), (0, 0))).reshape(
        B, nq, A_BLOCK, A_KV_HEADS, A_GROUP, A_HD)

    def key_blocks(a):
        a = jnp.pad(a.astype(F32), ((0, 0), (pad + A_BLOCK, 0), (0, 0), (0, 0))).reshape(
            B, nq + 1, A_BLOCK, A_KV_HEADS, A_HD)
        return jnp.concatenate([a[:, :-1], a[:, 1:]], axis=2)

    kb, vb = key_blocks(k), key_blocks(v)
    r = jnp.arange(A_BLOCK)
    c = jnp.arange(2 * A_BLOCK)
    dist = r[:, None] + A_BLOCK - c[None, :]
    kpos = (jnp.arange(nq)[:, None] - 1) * A_BLOCK - pad + c[None, :]
    valid = ((dist >= 0) & (dist < WINDOW))[None] & (kpos >= 0)[:, None, :]
    s = jnp.einsum('bnqhgd,bnkhd->bnhgqk', qb, kb) * (A_HD ** -0.5) + rel_bias_heads(rel_table, dist)
    s = jnp.where(valid[None, :, None, None], s, -jnp.inf)
    p = sink_softmax(s, sinks)
    o = jnp.einsum('bnhgqk,bnkhd->bnqhgd', p, vb).reshape(B, nq * A_BLOCK, A_WIDTH)
    return o[:, pad:].astype(q.dtype)

def swa_sample(q, k, v, cache_k, cache_v, sinks, rel_table):
    B, S = q.shape[:2]
    kk = jnp.concatenate([cache_k, k.astype(cache_k.dtype)], axis=1)
    vv = jnp.concatenate([cache_v, v.astype(cache_v.dtype)], axis=1)
    qpos = PAST_LEN + jnp.arange(S)
    kpos = jnp.concatenate([PAST_LEN - WINDOW + jnp.arange(WINDOW), PAST_LEN + jnp.arange(S)])
    dist = qpos[:, None] - kpos[None, :]
    valid = (dist >= 0) & (dist < WINDOW)
    qg = q.reshape(B, S, A_KV_HEADS, A_GROUP, A_HD).astype(F32)
    s = jnp.einsum('bqhgd,bkhd->bhgqk', qg, kk.astype(F32)) * (A_HD ** -0.5) + rel_bias_heads(rel_table, dist)
    s = jnp.where(valid, s, -jnp.inf)
    p = sink_softmax(s, sinks)
    o = jnp.einsum('bhgqk,bkhd->bqhgd', p, vv.astype(F32)).reshape(B, S, A_WIDTH)
    return o.astype(q.dtype), kk[:, -WINDOW:], vv[:, -WINDOW:]

def merge_groups(h_m, o_m, att, g_m, g_a, w_out):
    B, H, L, _ = h_m.shape
    hm = jnp.swapaxes(h_m, 1, 2).reshape(B, L, M_WIDTH).astype(o_m.dtype) * jax.nn.sigmoid(o_m)
    y = jnp.concatenate([rms_norm(hm, g_m), rms_norm(att, g_a)], axis=-1)
    return y @ w_out

def moe_ffn(x, w_router, b_router, w1, b1, w2, b2):
    xf = x.reshape(-1, D_MODEL)
    T = xf.shape[0]
    logits = (xf @ w_router + b_router).astype(F32)
    top_v, top_i = lax.top_k(logits, TOP_K)
    gates = jax.nn.softmax(top_v, axis=-1)
    A = T * TOP_K
    blk = max(8, min(MOE_BLOCK, A // N_EXPERTS))
    nb = -(-A // blk) + N_EXPERTS
    e_flat = top_i.reshape(-1)
    tok_flat = jnp.repeat(jnp.arange(T, dtype=jnp.int32), TOP_K)
    g_flat = gates.reshape(-1)
    order = jnp.argsort(e_flat, stable=True)
    e_s, tok_s, g_s = e_flat[order], tok_flat[order], g_flat[order]
    counts = jnp.bincount(e_flat, length=N_EXPERTS)
    starts = jnp.cumsum(counts) - counts
    padded = (counts + blk - 1) // blk * blk
    pends = jnp.cumsum(padded)
    dest = (pends - padded)[e_s] + jnp.arange(A) - starts[e_s]
    rows = nb * blk
    row_tok = jnp.full((rows,), T, jnp.int32).at[dest].set(tok_s)
    row_gate = jnp.zeros((rows,), F32).at[dest].set(g_s)
    blk_exp = jnp.minimum(jnp.searchsorted(pends, jnp.arange(nb) * blk, side='right'), N_EXPERTS - 1)

    def run_block(args):
        toks, gate, e = args
        xb = xf[jnp.minimum(toks, T - 1)]
        h = xb @ w1[e] + b1[e]
        x_glu = jnp.minimum(h[:, 0::2], SWIGLU_LIMIT)
        x_lin = jnp.clip(h[:, 1::2], -SWIGLU_LIMIT, SWIGLU_LIMIT)
        a = x_glu * jax.nn.sigmoid(SWIGLU_ALPHA * x_glu) * (x_lin + 1.0)
        y = a @ w2[e] + b2[e]
        return y.astype(F32) * gate[:, None]

    ys = lax.map(run_block, (row_tok.reshape(nb, blk), row_gate.reshape(nb, blk), blk_exp))
    out = jax.ops.segment_sum(ys.reshape(rows, D_MODEL), row_tok, num_segments=T + 1)[:T]
    return out.reshape(x.shape).astype(x.dtype)

def setup_inputs(seed: int = 0) -> dict:
    key = jax.random.key(seed)
    ks = jax.random.split(key, 26)
    nrm = lambda k, shape, scale: jax.random.normal(k, shape, F32) * scale
    return {
        'x_prompt': nrm(ks[0], (BATCH, SEQ, D_MODEL), 1.0),
        'x_sample': nrm(ks[1], (DEC_BATCH, DEC_SEQ, D_MODEL), 1.0),
        'cache_swa_k': nrm(ks[2], (DEPTH, DEC_BATCH, WINDOW, A_KV_HEADS, A_HD), 1.0),
        'cache_swa_v': nrm(ks[3], (DEPTH, DEC_BATCH, WINDOW, A_KV_HEADS, A_HD), 1.0),
        'state_mlstm_C': nrm(ks[4], (DEPTH, DEC_BATCH, M_HEADS, M_DV, M_DK), 0.5),
        'state_mlstm_n': nrm(ks[5], (DEPTH, DEC_BATCH, M_HEADS, M_DK), 0.5),
        'state_mlstm_m': nrm(ks[6], (DEPTH, DEC_BATCH, M_HEADS), 1.0),
        'meta_tokens': nrm(ks[7], (N_META, D_MODEL), 1.0),
        'rel_bias': nrm(ks[8], (REL_BUCKETS, A_HEADS), 0.5),
        'w_in': nrm(ks[9], (DEPTH, D_MODEL, N_IN), D_MODEL ** -0.5),
        'b_igate': nrm(ks[10], (DEPTH, M_HEADS), 0.1),
        'b_fgate': 3.0 + 3.0 * jax.random.uniform(ks[11], (DEPTH, M_HEADS), F32),
        'attn_sinks': nrm(ks[12], (DEPTH, A_HEADS), 0.5),
        'g_mlstm_out': 1.0 + nrm(ks[13], (DEPTH, M_WIDTH), 0.02),
        'g_attn_out': 1.0 + nrm(ks[14], (DEPTH, A_WIDTH), 0.02),
        'w_out': nrm(ks[15], (DEPTH, MIX_WIDTH, D_MODEL), DN_BETA * MIX_WIDTH ** -0.5),
        'ln1_g': 1.0 + nrm(ks[16], (DEPTH, D_MODEL), 0.02),
        'ln1_b': nrm(ks[17], (DEPTH, D_MODEL), 0.02),
        'w_router': nrm(ks[18], (DEPTH, D_MODEL, N_EXPERTS), D_MODEL ** -0.5),
        'b_router': nrm(ks[19], (DEPTH, N_EXPERTS), 0.01),
        'w_moe1': nrm(ks[20], (DEPTH, N_EXPERTS, D_MODEL, 2 * D_FF), D_MODEL ** -0.5),
        'b_moe1': nrm(ks[21], (DEPTH, N_EXPERTS, 2 * D_FF), 0.01),
        'w_moe2': nrm(ks[22], (DEPTH, N_EXPERTS, D_FF, D_MODEL), DN_BETA * D_FF ** -0.5),
        'b_moe2': nrm(ks[23], (DEPTH, N_EXPERTS, D_MODEL), 0.01),
        'ln2_g': 1.0 + nrm(ks[24], (DEPTH, D_MODEL), 0.02),
        'ln2_b': nrm(ks[25], (DEPTH, D_MODEL), 0.02),
    }

def reference(x_prompt, x_sample, cache_swa_k, cache_swa_v, state_mlstm_C, state_mlstm_n, state_mlstm_m,
              meta_tokens, rel_bias, w_in, b_igate, b_fgate, attn_sinks, g_mlstm_out, g_attn_out, w_out,
              ln1_g, ln1_b, w_router, b_router, w_moe1, b_moe1, w_moe2, b_moe2, ln2_g, ln2_b):
    B = x_prompt.shape[0]
    meta = jnp.broadcast_to(meta_tokens.astype(x_prompt.dtype)[None], (B, N_META, D_MODEL))
    xp = jnp.concatenate([meta, x_prompt], axis=1)
    xs = x_sample
    kp_l, vp_l, Cp_l, np_l, mp_l = [], [], [], [], []
    ks_l, vs_l, Cs_l, ns_l, ms_l = [], [], [], [], []
    for l in range(DEPTH):
        (qm, km, vm, ig, lf), om, (qa, ka, va) = split_projections(xp, w_in[l], b_igate[l], b_fgate[l])
        h, (C, n, m) = mlstm_prompt(qm, km, vm, ig, lf)
        att = swa_prompt(qa, ka, va, attn_sinks[l], rel_bias)
        mix = merge_groups(h, om, att, g_mlstm_out[l], g_attn_out[l], w_out[l])
        xp = layer_norm(DN_ALPHA * xp + mix, ln1_g[l], ln1_b[l])
        ff = moe_ffn(xp, w_router[l], b_router[l], w_moe1[l], b_moe1[l], w_moe2[l], b_moe2[l])
        xp = layer_norm(DN_ALPHA * xp + ff, ln2_g[l], ln2_b[l])
        kp_l.append(ka[:, -WINDOW:].astype(cache_swa_k.dtype))
        vp_l.append(va[:, -WINDOW:].astype(cache_swa_v.dtype))
        Cp_l.append(C.astype(state_mlstm_C.dtype))
        np_l.append(n.astype(state_mlstm_n.dtype))
        mp_l.append(m.astype(state_mlstm_m.dtype))
        (qm, km, vm, ig, lf), om, (qa, ka, va) = split_projections(xs, w_in[l], b_igate[l], b_fgate[l])
        st = (state_mlstm_C[l].astype(F32), state_mlstm_n[l].astype(F32), state_mlstm_m[l].astype(F32))
        (C, n, m), h = mlstm_chunk(st, (qm, km, vm, ig, lf))
        att, kbuf, vbuf = swa_sample(qa, ka, va, cache_swa_k[l], cache_swa_v[l], attn_sinks[l], rel_bias)
        mix = merge_groups(h, om, att, g_mlstm_out[l], g_attn_out[l], w_out[l])
        xs = layer_norm(DN_ALPHA * xs + mix, ln1_g[l], ln1_b[l])
        ff = moe_ffn(xs, w_router[l], b_router[l], w_moe1[l], b_moe1[l], w_moe2[l], b_moe2[l])
        xs = layer_norm(DN_ALPHA * xs + ff, ln2_g[l], ln2_b[l])
        ks_l.append(kbuf)
        vs_l.append(vbuf)
        Cs_l.append(C.astype(state_mlstm_C.dtype))
        ns_l.append(n.astype(state_mlstm_n.dtype))
        ms_l.append(m.astype(state_mlstm_m.dtype))
    y_prompt = xp[:, N_META:]
    y_sample = xs
    return (y_prompt, y_sample,
            jnp.stack(kp_l), jnp.stack(vp_l), jnp.stack(Cp_l), jnp.stack(np_l), jnp.stack(mp_l),
            jnp.stack(ks_l), jnp.stack(vs_l), jnp.stack(Cs_l), jnp.stack(ns_l), jnp.stack(ms_l))


_drawn_inputs = setup_inputs


def setup_inputs(seed=0):
    import zlib

    import numpy as np

    out = dict(_drawn_inputs(seed))
    spreads = {}
    factors = {'attn_sinks': 8.0,
     'g_mlstm_out': 11.581,
     'g_attn_out': 10.585,
     'b_router': 2.782,
     'b_moe1': 8.0,
     'b_moe2': 8.0,
     'ln2_g': 8.082,
     'ln2_b': 7.957}
    for name, (base, spread) in spreads.items():
        noise = np.random.default_rng([zlib.crc32(name.encode()), seed]).standard_normal(out[name].shape)
        drawn = base * np.exp(spread * noise) if base else spread * noise
        out[name] = jnp.asarray(drawn.astype(out[name].dtype))
    for name, factor in factors.items():
        out[name] = (out[name] * factor).astype(out[name].dtype)
    return out
```

```python
from contextlib import ExitStack

import numpy as np
import concourse.bass as bass
from concourse import mybir

ALU = mybir.AluOpType
ACT = mybir.ActivationFunctionType
F32 = mybir.dt.float32
I32 = mybir.dt.int32
U32 = mybir.dt.uint32
AX = mybir.AxisListType.X

P = 128
D = 1024
KT = D // P
SEQ, NS, NM = 512, 8, 16
NT = SEQ // P
META = 32
SM = META + NM
COLS = SEQ + SM
H, DV = 4, 128
HA, G, HD = 8, 4, 64
NB, B8 = 8, 8
E, TOPK = 32, 4
BLK = P
OVER = 16
NTOK = SEQ + NS
ALPHA = 2.0 ** 0.25
EPS = 1e-5
LIMIT, SWI = 7.0, 1.702
NEG = -1e30
BIG = 4096.0
CH = 256
RELW = 384
RING = 12
STREAM = 6
SLOT = [3, 4, 5, 0, 1, 2, 6, 7, 8, 9, 10, 11]
CHUNKS = [("o", 1536), ("o", 1792), ("kv", 2568), ("v", 1024), ("v", 1280), ("k", 512), ("k", 768),
          ("q", 0), ("q", 256), ("a", 2056), ("a", 2056)]


def small(tt):
    return tt == NT


def rows_of(tt):
    return SM if small(tt) else P


def cols_of(tt):
    return slice(P * tt, P * tt + rows_of(tt))


def projection_plan():
    units = []
    for tt in range(NT + 1):
        units += [("x", tt, 0, "act"), ("x", tt, 1, "dve")]
    for c, (kind, _) in enumerate(CHUNKS):
        if kind == "o":
            units += [("o", c, tt, "act") for tt in range(NT + 1)]
        elif kind == "kv":
            units += [("kv", c, tt, "dve") for tt in range(NT + 1)]
            units += [("g", 0, 0, "dve"), ("g", 0, 1, "dve")]
        elif kind == "v":
            units += [("v", c, tt, "act" if tt % 2 else "dve") for tt in range(NT + 1)]
        else:
            for m in range(2):
                units += [(kind, 2 * c + m, 0, "act"), (kind, 2 * c + m, 1, "dve")]
    units += [("gc", 0, 0, "dve"), ("ms", 0, 0, "dve")] + [("mb", h, 0, "dve") for h in range(H)]
    units += [("kn", h, 0, "act") for h in range(H)] + [("kns", 0, 0, "dve")]
    units += [("kaT", 0, 0, "act"), ("kaT", 1, 0, "dve"), ("qs", 0, 0, "dve")]
    units += [("st", h, 0, "dve") for h in range(H)]
    return units


PLAN = projection_plan()
BANKS_A = 6


def stream_incs(s):
    return 64 if s < len(CHUNKS) and CHUNKS[s][0] == "a" else 16


def streamed(s):
    return sum(stream_incs(t) for t in range(s % STREAM, s + 1, STREAM))


N_STREAM = len(CHUNKS) + 4
BEFORE = [sum(stream_incs(t) for t in range(s, N_STREAM, STREAM)) if s < STREAM else 0 for s in range(RING)]


def chunk_units(c):
    kind = CHUNKS[c][0]
    last = (kind, c, NT) if kind in ("o", "kv", "v") else (kind, 2 * c + 1, 1)
    return unit_index(*last) + 1


def emptied(n, engine):
    return sum(u[3] == engine for u in PLAN[:n])


def unit_index(*key):
    return [u[:3] for u in PLAN].index(key)


class Chain:

    def __init__(self, eng, sem):
        self.eng, self.sem, self.count, self.base, self.start, self.per_round = eng, sem, {}, {}, {}, {}

    def __call__(self, ins, sem=None, wait=True):
        s = self.sem if sem is None else sem
        self.count[s.name] = self.count.get(s.name, 0) + 1
        ins.then_inc(s, 1)
        if wait:
            self.eng.wait_ge(s, self.base.get(s.name, 0) + self.count[s.name])

    def loop(self, per_round):
        self.start = {s.name: self.count.get(s.name, 0) for s, _ in per_round}
        self.per_round = {s.name: n for s, n in per_round}

    def start_round(self, rnd):
        self.count = dict(self.start)
        self.base = {k: rnd * n for k, n in self.per_round.items()}

    def end_round(self):
        assert self.count == {k: self.start[k] + n for k, n in self.per_round.items()}, (self.count, self.start)


def decoder_layer(nc, x_prompt, x_sample, cache_k, cache_v, st_C, st_n, st_m, meta, rel_bias, w_in, b_ig, b_fg,
                  sinks, g_m, g_a, w_out, ln1_g, ln1_b, w_router, b_router, w1, b1, w2, b2, ln2_g, ln2_b,
                  consts, rel_consts,
                  y_prompt, y_sample, kp_out, vp_out, Cp_out, np_out, mp_out, ks_out, vs_out, Cs_out, ns_out, ms_out):
    x1_dram = nc.dram_tensor("x1_rows", (NTOK, D), F32).ap()
    y_dram = nc.dram_tensor("expert_rows", (NTOK * TOPK, D), F32).ap()
    band_dram = nc.dram_tensor("relative_bias_band", (HA, P, 2 * P), F32).ap()

    w_in_v = w_in.rearrange("o (k p) n -> p (o k) n", p=P)
    w_out_v = w_out.rearrange("o (k p) n -> p (o k) n", p=P)
    xp = x_prompt.rearrange("o (t p) d -> p (o t) d", p=P)
    ctx = ExitStack()
    with ctx:
        def sb(name, n, dt=F32):
            return ctx.enter_context(nc.sbuf_tensor(name, [P, n], dt))

        def sem(name):
            return ctx.enter_context(nc.semaphore(name))

        ring = ctx.enter_context(nc.sbuf_tensor("ring", [P, RING, 2048], F32))
        X = ctx.enter_context(nc.sbuf_tensor("X", [P, NT + 1, D], F32))
        mix = ctx.enter_context(nc.sbuf_tensor("mix", [P, NT + 1, D], F32))
        xT_t = sb("xT", KT * COLS)
        qmT = ctx.enter_context(nc.sbuf_tensor("qmT", [P, H, COLS], F32))
        kmT = ctx.enter_context(nc.sbuf_tensor("kmT", [P, H, COLS], F32))
        kn = ctx.enter_context(nc.sbuf_tensor("kn", [P, NT + 1, 512], F32))
        vaug = ctx.enter_context(nc.sbuf_tensor("vaug", [P, NT + 1, H * (DV + 1)], F32))
        kva = ctx.enter_context(nc.sbuf_tensor("kva", [P, NT + 1, CH], F32))
        kaT = sb("kaT", COLS)
        cst = ctx.enter_context(nc.sbuf_tensor("cst", [P, 4, P], F32))
        ident, strict, causal, ones = (cst[:, i, :] for i in range(4))
        GC = ctx.enter_context(nc.sbuf_tensor("GC", [P, NT + 1, 68], F32))
        sm_t = sb("smalls", 1120)
        small_at = [0]

        def sml(n, rows=P):
            a = small_at[0]
            small_at[0] += n
            assert small_at[0] <= 1120
            return sm_t[0:rows, a:a + n]

        def chunk(s):
            return ring[:, s, :].rearrange("p (k n) -> p k n", k=KT)

        def rowpair(s):
            return ring[:, s, :].rearrange("p (k n) -> p k n", k=2)

        xT = xT_t[:, :].rearrange("p (k n) -> p k n", k=KT)
        qaT = ring[:, 6, :].rearrange("p (c n) -> p c n", c=4)
        Cst = ring[:, 7:9, :].rearrange("p s n -> p (s n)").rearrange("p (i d) -> p i d", d=DV)
        cK = ring[:, 9, 0:1024].rearrange("p (b n) -> p b n", b=NS)
        cV = ring[:, 9, 1024:2048].rearrange("p (b n) -> p b n", b=NS)
        KTs = ring[:, 10, 0:1024].rearrange("p (b n) -> p b n", b=NS)
        qs = ring[0:NS, 10, 0:512]
        vm = ring[0:NS, 10, 512:1024]
        vms = [vm, ring[0:NS, 11, 516:1028]]
        ST = ring[0:68, 10, 1024:1024 + COLS]
        wgp = ring[:, 10, 1584:1584 + 288].rearrange("p (k n) -> p k n", k=KT)
        wgs = ring[:, 10, 1872:1936].rearrange("p (k n) -> p k n", k=KT)
        ra, rb, rc = (ring[0:4, 11, COLS * i:COLS * (i + 1)] for i in range(3))
        WV, CT, NUM = (ring[:, 11, 516 * i:516 * (i + 1)].rearrange("p (h c) -> p h c", h=H) for i in range(3))
        Ssb = ring[:, 11, :].rearrange("p (h n) -> p h n", h=HA)
        Pm = xT_t[:, 0:2048].rearrange("p (h n t) -> p h n t", h=H, n=NT)
        PTa = xT_t[:, 0:2048].rearrange("p (k q) -> p k q", q=P)
        band = xT_t[:, 2048:4096].rearrange("p (h n) -> p h n", h=HA)
        wr = xT_t[:, 4096:4352].rearrange("p (k n) -> p k n", k=KT)
        br = xT_t[:, 4352:4384]
        mixT = [qmT[:, :, :].rearrange("p h n -> p (h n)")[:, 1024 * i:1024 * (i + 1)].rearrange("p (k n) -> p k n", k=KT)
                for i in range(2)]
        lng = kmT[:, :, :].rearrange("p h n -> p (h n)")[:, 0:1024]
        lnb = kmT[:, :, :].rearrange("p h n -> p (h n)")[:, 1024:2048]
        knf = kn[:, :, :].rearrange("p t n -> p (t n)")
        rel_c = knf[0:E, 0:2 * RELW]
        relx = knf[0:HA, 2 * RELW:3 * RELW]
        relt = knf[0:E, 3 * RELW:3 * RELW + HA]
        b1rows = knf[0:E, 0:2048]
        b1T = knf[:, 2048:2560].rearrange("p (c e) -> p c e", e=E)
        mf = mix[:, :, :].rearrange("p t n -> p (t n)")
        xg = mf[:, 0:1024]
        xgT = mf[:, 1024:2048].rearrange("p (k n) -> p k n", k=KT)
        aT = mf[:, 2048:3072].rearrange("p (k n) -> p k n", k=KT)
        ysb = mf[:, 3072:4096]
        ht = mf[:, 4096:4608].rearrange("p (c n) -> p c n", c=4)
        gt = mf[:, 4608:4864].rearrange("p (c n) -> p c n", c=2)
        lt = mf[:, 4864:5120].rearrange("p (c n) -> p c n", c=2)
        sg = kaT[:, 0:256].rearrange("p (c n) -> p c n", c=2)
        vf = vaug[:, :, :].rearrange("p t n -> p (t n)")
        PS1 = vf[:, 0:640].rearrange("p (t n) -> p t n", n=P)
        iota = vf[:, 640:1408]
        T2 = vf[:, 1408:1728].rearrange("p (t e c) -> p t e c", e=E, c=2)
        RK = vf[:, 1728:1888].rearrange("p (t e) -> p t e", e=E)
        SEL = vf[:, 1888:2048].rearrange("p (t e) -> p t e", e=E)
        LG = vf[:, 2048:2208].rearrange("p (t e) -> p t e", e=E)
        GT_ = vf[:, 2208:2368].rearrange("p (t e) -> p t e", e=E)
        OH = xT_t[:, 0:640].rearrange("p (t k e) -> p t k e", k=TOPK, e=E)
        OG = xT_t[:, 640:1280].rearrange("p (t k e) -> p t k e", k=TOPK, e=E)
        cmpq = xT_t[0:1, 1280:1280 + OVER * E].rearrange("p (q e) -> p q e", e=E)
        cmpo = xT_t[0:1, 1792:1792 + OVER * E].rearrange("p (q e) -> p q e", e=E)
        Yt = [ring[:, 2 * i:2 * i + 2, :].rearrange("p s n -> p (s n)").rearrange("p (k n) -> p k n", k=TOPK)
              for i in range(2)]
        b2sb = ring[0:E, 4, 0:1024]
        GTT = ring[0:E, 5, 0:NTOK]
        zb = [ring[:, 6 + i, 0:1024] for i in range(2)]

        qaS = sml(4 * NS).rearrange("p (c b) -> p c b", c=4)
        Me = sml(5 * H).rearrange("p (n h) -> p n h", h=H)
        wg = sml(5 * H).rearrange("p (n h) -> p n h", h=H)
        dec = sml(NT * H).rearrange("p (n h) -> p n h", h=H)
        wint = sml(NT * H).rearrange("p (n h) -> p n h", h=H)
        emt = sml(NT * H).rearrange("p (n h) -> p n h", h=H)
        big_b = sml(1)
        bf_b = sml(1)
        SEx = ring[0:64, 11, 1548:1676]
        xsq = ring[:, 11, 0:512]
        nsb = mix[0:NS, NT, 512:1024]
        gcol = sml(8)
        sinkb = sml(8)
        den4 = sml(8)
        mx8 = sml(8)
        nmx8 = sml(8)
        sum8 = sml(8)
        esk = sml(8)
        sm_st, smt, sa, sw, s_em, sd = (sml(4, NS) for _ in range(6))
        nfin = sml(128, 4)
        tok4 = sml(5)
        sden = sml(4, NS)
        Asel = sml(32, NS).rearrange("p (b h) -> p b h", h=H)
        abc = sml(32).rearrange("p (b h) -> p b h", h=H)
        NUMS = sml(32).rearrange("p (b h) -> p b h", h=H)
        STs = sml(64)
        PTs = sml(64)
        bSs = sml(128, 64)
        sks = sml(4, 64)
        OTs = sml(64, 64)
        ss2 = sml(2)
        rs2 = sml(2)
        powc = sml(4)
        bst = sml(12)
        bag = sml(4)
        rstd = sml(1)
        nbias = sml(1)
        top8 = sml(40).rearrange("p (t k) -> p t k", k=8)
        idx8 = sml(40).rearrange("p (t k) -> p t k", k=8)
        idxf = sml(20).rearrange("p (t k) -> p t k", k=TOPK)
        gat = sml(20).rearrange("p (t k) -> p t k", k=TOPK)
        ntop = sml(5)
        gsum = sml(5)
        tokid = sml(5)
        v3 = sml(15).rearrange("p (t c) -> p t c", c=3)
        b1c = sml(16)
        nxt = sml(4)
        cur = sml(4)
        nxi, cui = nxt.bitcast(I32), cur.bitcast(I32)
        cntf = sml(32)
        ovf = sml(32, 1)
        cum = sml(32, 1)
        tabf = xT_t[0:1, 2400:2596].rearrange("p (j c) -> p j c", c=4)
        tabi = ctx.enter_context(nc.sbuf_tensor("tabi", [1, 4 * 49 + 4], I32))
        tab = tabi[:, 0:196].rearrange("p (j c) -> p j c", c=4)

        PS = ctx.enter_context(nc.psum_tensor("PS", [P, 8, 512], F32))

        def bank(i):
            return PS[:, i, :]

        def heads(b0):
            return PS[:, b0:b0 + 2, :].rearrange("p b (h c) -> p (b h) c", c=256)[:, :, 0:DV + 1]

        cst_in, rel_in, relw_out, band_in, wg_in, gb_in = (sem(n) for n in ("cst_in", "rel_in", "relw_out", "band_in", "wg_in", "gb_in"))
        ch_in, cv_in, cnew_in, bs_in, sc_in, sn_in = (sem(n) for n in ("ch_in", "cv_in", "cnew_in", "bs_in", "sc_in", "sn_in"))
        sm_in, router_in, ln_in, b1_in, b2_in, ln2_in = (sem(n) for n in ("sm_in", "router_in", "ln_in", "b1_in", "b2_in", "ln2_in"))
        zeroed, prompt_C_out, ns_done, shift_out, state_out, x1_out = (sem(n) for n in ("zeroed", "prompt_C_out", "ns_done", "shift_out", "state_out", "x1_out"))
        fin_state, unit_mm, unit_act, unit_dve, dve_chain, act_chain = (sem(n) for n in ("fin_state", "unit_mm", "unit_act", "unit_dve", "dve_chain", "act_chain"))
        pool_chain, rel_mm, rel_done, wg_ready, gate_abs, gate_ln = (sem(n) for n in ("pool_chain", "rel_mm", "rel_done", "wg_ready", "gate_abs", "gate_ln"))
        gate_rows, col_gates, exp_gates, exp_intra, wv_ready, state_mm = (sem(n) for n in ("gate_rows", "col_gates", "exp_gates", "exp_intra", "wv_ready", "state_mm"))
        out_mm, state_ready, chunk_read, fin_mm, fin_copied, s_gates = (sem(n) for n in ("out_mm", "state_ready", "chunk_read", "fin_mm", "fin_copied", "s_gates"))
        s_exp, s_sel, s_amm, s_vm, s_outer, s_num = (sem(n) for n in ("s_exp", "s_sel", "s_amm", "s_vm", "s_outer", "s_num"))
        s_numt, s_hdone, sk_mm, sk_cp, ss_mm, ss_cp = (sem(n) for n in ("s_numt", "s_hdone", "sk_mm", "sk_cp", "ss_mm", "ss_cp"))
        st_mm, s_max, s_aexp, s_pn, sp_mm, sp_cp = (sem(n) for n in ("st_mm", "s_max", "s_aexp", "s_pn", "sp_mm", "sp_cp"))
        so_mm, so_cp, sot_mm, s_att, at_mm, at_max = (sem(n) for n in ("so_mm", "so_cp", "sot_mm", "s_att", "at_mm", "at_max"))
        at_exp, at_tr, at_pt, at_pv, at_out, sq_done = (sem(n) for n in ("at_exp", "at_tr", "at_pt", "at_pv", "at_out", "sq_done"))
        rms_pow, rms_scaled, mt_mm, mt_cp, op_mm, ln_stat = (sem(n) for n in ("rms_pow", "rms_scaled", "mt_mm", "mt_cp", "op_mm", "ln_stat"))
        ln_pow, ln_nb, ln_norm, x1_done, x1_mm, x1_cp = (sem(n) for n in ("ln_pow", "ln_nb", "ln_norm", "x1_done", "x1_mm", "x1_cp"))
        lg_mm, lg_done, b1_mm, b1_cp, iota_done, top_done = (sem(n) for n in ("lg_mm", "lg_done", "b1_mm", "b1_cp", "iota_done", "top_done"))
        gexp_done, sel_ready, rank_mm, tab_ready, p_ready, idx_mm = (sem(n) for n in ("gexp_done", "sel_ready", "rank_mm", "tab_ready", "p_ready", "idx_mm"))
        idx_ready, xg_in, xt_mm, xt_ready, chunk_used, h_read = (sem(n) for n in ("idx_ready", "xg_in", "xt_mm", "xt_ready", "chunk_used", "h_read"))
        g_ready, sig_ready, a_ready, y_read, y_out, cur_ready = (sem(n) for n in ("g_ready", "sig_ready", "a_ready", "y_read", "y_out", "cur_ready"))
        gt_mm, gt_cp, b2_mm, y_half, f_stat = (sem(n) for n in ("gt_mm", "gt_cp", "b2_mm", "y_half", "f_stat"))
        f_pow, f_nb, f_norm, f_done, yt_used, f_chain = (sem(n) for n in ("f_pow", "f_nb", "f_norm", "f_done", "yt_used", "f_chain"))
        s_abc, s_scaled, b2_read = sem("s_abc"), sem("s_scaled"), sem("b2_read")
        sync_steps, pool_steps = sem("sync_steps"), sem("pool_steps")
        x_in = [sem(f"x_in{i}") for i in range(NT + 1)]
        slot_in = [sem(f"slot_in{i}") for i in range(RING)]
        yt_in = [sem("yt_in0"), sem("yt_in1")]
        fin_out = [sem("fin_out0"), sem("fin_out1")]

        block = ctx.enter_context(nc.Block())

        def moe_landed(c, j):
            return j * 16 + (BEFORE[SLOT[c]] + 16)

        @block.sync
        def _(sp):
            for tt in range(NT):
                sp.dma_start(X[:, tt, :], xp[:, tt, :]).then_inc(x_in[tt], 16)
            sp.wait_ge(zeroed, 1)
            sp.dma_start(X[0:NS, NT, :], x_sample.rearrange("b o d -> (b o) d")).then_inc(x_in[NT], 16)
            sp.dma_start(X[META:SM, NT, :], meta).then_inc(x_in[NT], 16)
            for s, (kind, col) in enumerate(CHUNKS):
                if s >= STREAM:
                    sp.wait_ge(unit_mm, chunk_units(s - STREAM))
                if kind != "a":
                    sp.dma_start(chunk(s % STREAM), w_in_v[:, :, col:col + CH]).then_inc(slot_in[s % STREAM], 16)
                else:
                    first = 2 * (s - len(CHUNKS) + 2)
                    for m in range(2):
                        for kv in range(2):
                            a = col + HD * (first + m + G * kv)
                            sp.dma_start(chunk(s % STREAM)[:, :, P * m + HD * kv:P * m + HD * kv + HD],
                                         w_in_v[:, :, a:a + HD]).then_inc(slot_in[s % STREAM], 16)
            for i in range(4):
                s = len(CHUNKS) + i
                sp.wait_ge(unit_mm, chunk_units(s - STREAM))
                sp.dma_start(rowpair(s % STREAM), w_out_v[:, 2 * i:2 * i + 2, :]).then_inc(slot_in[s % STREAM], 16)

            def load_chunk(e, c):
                s = SLOT[c]
                if c < 8:
                    sp.dma_start(chunk(s), w1[0, bass.ds(e, 1), :, CH * c:CH * c + CH].rearrange(
                        "e (k p) n -> p (e k) n", p=P)).then_inc(slot_in[s], 16)
                else:
                    d = c - 8
                    sp.dma_start(rowpair(s), w2[0, bass.ds(e, 1), 2 * P * d:2 * P * d + 2 * P, :].rearrange(
                        "e (k p) n -> p (e k) n", p=P)).then_inc(slot_in[s], 16)

            for c in range(2):
                sp.wait_ge(unit_mm, chunk_units(9 + c))
                load_chunk(0, c)
            sp.wait_ge(op_mm, NT + 1)
            for c in range(2, 6):
                load_chunk(0, c)
            sp.wait_ge(at_out, NT)
            sp.wait_ge(s_att, 1)
            sp.wait_ge(state_out, 16 * 7)
            sp.wait_ge(prompt_C_out, 32)
            for c in range(6, 12):
                load_chunk(0, c)
            with sp.Fori(1, E) as j:
                for c in range(12):
                    sp.wait_ge(chunk_used, j * 12 + (c - 11))
                    load_chunk(j, c)
            sp.wait_ge(tab_ready, 1)
            n_over = sp.value_load(tabi[0:1, 196:197], min_val=0, max_val=OVER)
            with sp.Fori(0, OVER) as q:
                with sp.If(q < n_over):
                    e = sp.value_load(tab[0:1, bass.ds(q + E, 1), 0], min_val=0, max_val=E - 1)
                    for c in range(12):
                        sp.wait_ge(chunk_used, q * 12 + (E * 12 + c - 11))
                        load_chunk(e, c)
            blocks = n_over + E
            sp.wait_ge(y_out, blocks * 16 + 16)
            sp.sem_inc(sync_steps, 1)
            sp.wait_ge(chunk_used, blocks * 12)
            sp.sem_inc(sync_steps, 1)
            sp.wait_ge(xg_in, blocks * 16 + 16)
            sp.wait_ge(shift_out, 32)
            yv = y_dram.rearrange("(t k) n -> t k n", k=TOPK)
            sp.dma_start(b2sb, b2.rearrange("o e n -> (o e) n")).then_inc(b2_in, 16)

            def load_rows(tt):
                r = NS if small(tt) else P
                sp.dma_start(Yt[tt % 2][0:r], yv[P * tt:P * tt + r]).then_inc(yt_in[tt % 2], 16)

            load_rows(0)
            load_rows(1)
            for tt in range(NT + 1):
                if tt + 2 <= NT:
                    sp.wait_ge(yt_used, tt + 1)
                    load_rows(tt + 2)
                sp.wait_ge(f_done, tt + 1)
                if small(tt):
                    sp.dma_start(y_sample.rearrange("b o d -> (b o) d"), zb[tt % 2][0:NS, :]).then_inc(fin_out[tt % 2], 16)
                else:
                    sp.dma_start(y_prompt[0, P * tt:P * tt + P, :], zb[tt % 2]).then_inc(fin_out[tt % 2], 16)
            sp.wait_ge(fin_out[0], 48)
            sp.wait_ge(fin_out[1], 32)

        @block.gpsimd
        def _(pool):
            link = Chain(pool, pool_chain)
            dma = pool.dma_start
            dma(cst[:, 0:4, :], consts.rearrange("p (i n) -> p i n", i=4)).then_inc(cst_in, 16)
            dma(nxt[0:1, 3:4], consts[0:1, 0:1]).then_inc(y_out, 16)
            dma(rel_c, rel_consts).then_inc(rel_in, 16)
            dma(relt, rel_bias).then_inc(rel_in, 16)
            with nc.allow_non_contiguous_dma(reason="a few small columns"):
                dma(wgs, w_in_v[:, :, 2048:2056]).then_inc(wg_in, 16)
                dma(big_b[0:4, :], b_ig.rearrange("o h -> h o")).then_inc(gb_in, 16)
                dma(bf_b[32:36, :], b_fg.rearrange("o h -> h o")).then_inc(gb_in, 16)
                dma(gcol[:, 0:4], g_m.rearrange("o (c p) -> p (o c)", p=P)).then_inc(gb_in, 16)
                dma(gcol[:, 4:8], g_a.rearrange("o (c p) -> p (o c)", p=P)).then_inc(gb_in, 16)
                dma(sinkb, bass.AP(sinks.tensor, 0, [[0, P], [1, HA]])).then_inc(gb_in, 16)
                for kv in range(2):
                    for b in range(NS):
                        r0 = 32 * kv + G * b
                        dma(sks[r0:r0 + G, 0:1], bass.AP(sinks.tensor, G * kv, [[1, G], [1, 1]])).then_inc(gb_in, 16)
            dma(sm_st, st_m.rearrange("o b h -> (o b) h")).then_inc(sm_in, 16)
            dma(nsb, st_n.rearrange("o b h d -> (o b) (h d)")).then_inc(sn_in, 16)
            dma(Cst, st_C.rearrange("o b h v d -> v (o b h) d")).then_inc(sc_in, 16)
            dma(cK[0:P - 1], cache_k[0, :, 1:P].rearrange("b k h d -> k b (h d)")).then_inc(ch_in, 16)
            dma(cV[0:P - 1], cache_v[0, :, 1:P].rearrange("b k h d -> k b (h d)")).then_inc(cv_in, 16)
            dma(ks_out[0, :, 0:P - 1].rearrange("b k h d -> b k (h d)"),
                cache_k[0, :, 1:P].rearrange("b k h d -> b k (h d)")).then_inc(shift_out, 16)
            dma(vs_out[0, :, 0:P - 1].rearrange("b k h d -> b k (h d)"),
                cache_v[0, :, 1:P].rearrange("b k h d -> b k (h d)")).then_inc(shift_out, 16)
            pool.wait_ge(rel_done, 1)
            dma(band_dram, bass.AP(relx.tensor, relx.offset + P - 1, [list(relx.ap[0]), [-1, P], [1, 2 * P]])).then_inc(relw_out, 16)
            pool.wait_ge(unit_dve, emptied(unit_index("kv", 2, NT) + 1, "dve"))
            for b in range(NS):
                dma(cK[P - 1:P, b, :], kva[b:b + 1, NT, 0:P]).then_inc(cnew_in, 16)
                dma(cV[P - 1:P, b, :], kva[b:b + 1, NT, P:2 * P]).then_inc(cnew_in, 16)
            dma(ks_out[0, :, P - 1].rearrange("b h d -> b (h d)"), kva[0:NS, NT, 0:P]).then_inc(state_out, 16)
            dma(vs_out[0, :, P - 1].rearrange("b h d -> b (h d)"), kva[0:NS, NT, P:2 * P]).then_inc(state_out, 16)
            dma(kp_out[0, 0].rearrange("k h d -> k (h d)"), kva[:, NT - 1, 0:P]).then_inc(state_out, 16)
            dma(vp_out[0, 0].rearrange("k h d -> k (h d)"), kva[:, NT - 1, P:2 * P]).then_inc(state_out, 16)
            pool.wait_ge(gate_rows, 1)
            dma(mp_out.rearrange("o b h -> h (o b)"), ST[64:68, SEQ - 1:SEQ]).then_inc(state_out, 16)
            pool.wait_ge(unit_mm, chunk_units(len(CHUNKS) - 1))
            pool.wait_ge(relw_out, 16)
            dma(band, band_dram.rearrange("h r c -> r h c")).then_inc(band_in, 16)
            for kv in range(2):
                for b in range(NS):
                    r0 = 32 * kv + G * b
                    dma(bSs[r0:r0 + G, :], band_dram[G * kv:G * kv + G, P - 1, P:2 * P]).then_inc(bs_in, 16)
            dma(wr, w_router.rearrange("o (k p) n -> p (o k) n", p=P)).then_inc(router_in, 16)
            dma(br, bass.AP(b_router.tensor, 0, [[0, P], [1, E]])).then_inc(router_in, 16)
            pool.wait_ge(s_gates, 1)
            dma(ms_out.rearrange("o b h -> (o b) h"), smt).then_inc(state_out, 16)
            pool.wait_ge(fin_copied, 1)
            dma(Cp_out.rearrange("o b h v d -> v (o b h) d"), WV.rearrange("p h c -> p (h c)")[:, 0:512].rearrange(
                "p (h d) -> p h d", h=H)).then_inc(prompt_C_out, 16)
            dma(np_out.rearrange("o b h d -> (o b h) d"), nfin).then_inc(prompt_C_out, 16)
            pool.wait_ge(s_abc, 1)
            pool.wait_ge(sc_in, 16)
            for b in range(NS):
                Cb = Cst[:, H * b:H * b + H, :]
                nc.gpsimd.tensor_tensor(Cb, Cb, abc[:, b, :].unsqueeze(2).to_broadcast([P, H, DV]),
                                        ALU.mult).then_inc(s_scaled, 1)
            pool.wait_ge(s_hdone, 1)
            dma(ns_out.rearrange("o b h d -> (o b) (h d)"), nsb).then_inc(ns_done, 16)
            dma(Cs_out.rearrange("o b h v d -> v (o b h) d"), Cst).then_inc(state_out, 16)
            dma(lng, bass.AP(ln1_g.tensor, 0, [[0, P], [1, D]])).then_inc(ln_in, 16)
            dma(lnb, bass.AP(ln1_b.tensor, 0, [[0, P], [1, D]])).then_inc(ln_in, 16)
            dma(b1rows, b1.rearrange("o e n -> (o e) n")).then_inc(b1_in, 16)
            nc.gpsimd.memset(powc, -0.5).then_inc(pool_chain, 1)
            link.count[pool_chain.name] = 1
            nc.gpsimd.iota(iota, [[1, 768]], base=0, channel_multiplier=0, allow_small_or_imprecise_dtypes=True)
            nc.gpsimd.iota(tokid, [[P, NT + 1]], base=0, channel_multiplier=1,
                           allow_small_or_imprecise_dtypes=True).then_inc(iota_done, 1)
            def rms_power(tt):
                r = NS if small(tt) else P
                pool.wait_ge(sq_done, tt + 1)
                link(nc.gpsimd.tensor_scalar(rs2[0:r], ss2[0:r], 1.0 / 512, EPS, ALU.mult, ALU.add))
                nc.gpsimd.tensor_tensor(rs2[0:r], rs2[0:r], powc[0:r, 0:2], ALU.pow).then_inc(rms_pow, 1)

            rms_power(0)
            for tt in range(NT + 1):
                r = NS if small(tt) else P
                if tt < NT:
                    rms_power(tt + 1)
                pool.wait_ge(ln_stat, tt + 1)
                link(nc.gpsimd.tensor_scalar(rstd[0:r], bag[0:r, 1:2], 1.0, EPS, ALU.mult, ALU.add))
                nc.gpsimd.tensor_tensor(rstd[0:r], rstd[0:r], powc[0:r, 0:1], ALU.pow).then_inc(ln_pow, 1)
                pool.wait_ge(x1_done, tt + 1)
                dma(x1_dram[P * tt:P * tt + r, :], X[0:r, tt, :]).then_inc(x1_out, 16)
            dma(lng, bass.AP(ln2_g.tensor, 0, [[0, P], [1, D]])).then_inc(ln2_in, 16)
            dma(lnb, bass.AP(ln2_b.tensor, 0, [[0, P], [1, D]])).then_inc(ln2_in, 16)

            def gather(j):
                pool.wait_ge(idx_ready, j + 1)
                if not isinstance(j, int) or j > 0:
                    pool.wait_ge(xt_mm, j)
                pool.sem_inc(pool_steps, 1)
                nc.gpsimd.indirect_dma_start(out=xg, out_offset=None, in_=x1_dram, in_offset=bass.IndirectOffsetOnAxis(
                    ap=nxi[:, 0:1].bitcast(U32), axis=0)).then_inc(xg_in, 16)

            def scatter(j):
                pool.wait_ge(y_read, j + 2)
                pool.sem_inc(pool_steps, 1)
                nc.gpsimd.indirect_dma_start(out=y_dram, out_offset=bass.IndirectOffsetOnAxis(
                    ap=cui[:, 1:2].bitcast(U32), axis=0), in_=ysb, in_offset=None,
                    bounds_check=NTOK * TOPK - 1, oob_is_err=False).then_inc(y_out, 16)

            pool.wait_ge(x1_out, 16 * (NT + 1))
            gather(0)
            with pool.Fori(0, E) as j:
                gather(j + 1)
                scatter(j)
            n_over = pool.value_load(tabi[0:1, 196:197], min_val=0, max_val=OVER)
            with pool.Fori(0, OVER) as q:
                with pool.If(q < n_over):
                    gather(q + (E + 1))
                    scatter(q + E)

            def expert_pairs(tt):
                r = NS if small(tt) else P
                Y = Yt[tt % 2]
                pool.wait_ge(yt_in[tt % 2], 16 * (tt // 2 + 1))
                nc.gpsimd.tensor_tensor(Y[0:r, 0:4:2, :], Y[0:r, 0:4:2, :], Y[0:r, 1:4:2, :], ALU.add).then_inc(y_half, 1)

            expert_pairs(0)
            for tt in range(NT + 1):
                r = NS if small(tt) else P
                pool.wait_ge(f_stat, tt + 1)
                link(nc.gpsimd.tensor_scalar(rstd[0:r], bag[0:r, 1:2], 1.0, EPS, ALU.mult, ALU.add))
                nc.gpsimd.tensor_tensor(rstd[0:r], rstd[0:r], powc[0:r, 0:1], ALU.pow).then_inc(f_pow, 1)
                if tt < NT:
                    expert_pairs(tt + 1)

        @block.scalar
        def _(act):
            link = Chain(act, act_chain)
            for u, (kind, a, b, who) in enumerate(PLAN):
                if who != "act":
                    continue
                if kind == "kn" and a == 0:
                    act.wait_ge(relw_out, 16)
                act.wait_ge(unit_mm, u + 1)
                src = bank(u % BANKS_A)
                if kind == "x":
                    r = rows_of(a)
                    ins = nc.scalar.copy(xT[:, 4 * b:4 * b + 4, cols_of(a)],
                                         src.rearrange("p (k n) -> p k n", n=P)[:, :, 0:r])
                elif kind == "o":
                    r = rows_of(b)
                    ins = nc.scalar.activation(mix[0:r, b, CH * a:CH * a + CH], src[0:r, 0:CH], ACT.Sigmoid)
                elif kind == "v":
                    r = rows_of(b)
                    h0 = 2 * (a - 3)
                    ins = nc.scalar.copy(vaug[0:r, b, :].rearrange("p (h c) -> p h c", h=H)[:, h0:h0 + 2, 0:DV],
                                         src[0:r, 0:CH].rearrange("p (h c) -> p h c", h=2))
                elif kind == "k":
                    ins = nc.scalar.mul(kmT[:, a - 10, 0:SEQ], src, float(DV) ** -0.5)
                elif kind == "q":
                    ins = nc.scalar.copy(qmT[:, a - 14, 0:SEQ], src)
                elif kind == "a":
                    ins = nc.scalar.copy(qaT[:, a - 18, :], src)
                elif kind == "kn":
                    ins = nc.scalar.copy(kn[:, 0:NT, DV * a:DV * a + DV], src.rearrange("p (t n) -> p t n", t=NT))
                elif kind == "kaT":
                    ins = nc.scalar.copy(kaT[:, 0:SEQ], src)
                ins.then_inc(unit_act, 1)
                if (kind, a, b) == ("v", 3, 3):
                    act.wait_ge(gate_abs, 1)
                    link(nc.scalar.activation(rc, rc, ACT.Exp, scale=-1.0))
                    nc.scalar.activation(rc, rc, ACT.Ln, bias=1.0).then_inc(gate_ln, 1)
                if (kind, a, b) == ("kn", 3, 0):
                    act.wait_ge(col_gates, 1)
                    for gt4 in (wg[:, 0:NT, :], wg[META:SM, NT, :], dec, wint, emt):
                        ins = nc.scalar.activation(gt4, gt4, ACT.Exp)
                    ins.then_inc(exp_gates, 1)
                    for h in range(H):
                        for n in range(NT):
                            ins = nc.scalar.activation(Pm[:, h, n, :], Pm[:, h, n, :], ACT.Exp, bias=GC[:, n, h:h + 1])
                        ins.then_inc(exp_intra, 1)
            act.wait_ge(s_gates, 1)
            nc.scalar.activation(sa, sa, ACT.Exp)
            nc.scalar.activation(sw, sw, ACT.Exp)
            nc.scalar.activation(s_em, smt, ACT.Exp, scale=-1.0).then_inc(s_exp, 1)
            act.wait_ge(sk_mm, 1)
            act.wait_ge(s_hdone, 1)
            for i in range(2):
                ins = nc.scalar.copy(KTs[:, 4 * i:4 * i + 4, :], bank(i).rearrange("p (b n) -> p b n", b=4))
            ins.then_inc(sk_cp, 1)
            act.wait_ge(s_max, 1)
            nc.scalar.activation(SEx, SEx, ACT.Exp, bias=sks[:, 1:2], accum_out=sks[:, 2:3])
            nc.scalar.activation(sks[:, 3:4], sks[:, 0:1], ACT.Exp, bias=sks[:, 1:2]).then_inc(s_aexp, 1)
            for n in range(NT):
                for half in range(2):
                    act.wait_ge(at_max, 2 * n + half + 1)
                    for h in range(4 * half, 4 * half + 4):
                        nc.scalar.activation(Ssb[:, h, :], Ssb[:, h, :], ACT.Exp, bias=nmx8[:, h:h + 1],
                                             accum_out=sum8[:, h:h + 1])
                    hs = slice(4 * half, 4 * half + 4)
                    nc.scalar.activation(esk[:, hs], esk[:, hs], ACT.Exp).then_inc(at_exp, 1)
                for half in range(2):
                    act.wait_ge(at_tr, 2 * n + half + 1)
                    kk = 8 * half
                    v = PS[:, 4 + 2 * half:6 + 2 * half, :].rearrange("p b (k q) -> p (b k) q", q=P)
                    if n == 0:
                        nc.scalar.copy(PTa[0:SM, kk:kk + 8:2, :], v[0:SM, 0::2, :])
                        nc.scalar.copy(PTa[:, kk + 1:kk + 8:2, :], v[:, 1::2, :]).then_inc(at_pt, 1)
                    else:
                        nc.scalar.copy(PTa[:, kk:kk + 8, :], v).then_inc(at_pt, 1)
            act.wait_ge(at_out, NT)
            act.wait_ge(s_att, 1)
            def group_norms(tt):
                r = NS if small(tt) else P
                for g in range(2):
                    ins = nc.scalar.activation(xsq[0:r, :], mix[0:r, tt, 512 * g:512 * g + 512], ACT.Square,
                                               accum_out=ss2[0:r, g:g + 1])
                    link(ins) if g == 0 else ins.then_inc(sq_done, 1)
                act.wait_ge(rms_pow, tt + 1)
                nc.scalar.mul(mix[0:r, tt, 0:512], mix[0:r, tt, 0:512], rs2[0:r, 0:1])
                nc.scalar.mul(mix[0:r, tt, 512:1024], mix[0:r, tt, 512:1024], rs2[0:r, 1:2]).then_inc(rms_scaled, 1)

            group_norms(0)
            for tt in range(NT + 1):
                r = NS if small(tt) else P
                if tt < NT:
                    group_norms(tt + 1)
                act.wait_ge(ln_nb, tt + 1)
                nc.scalar.activation(X[0:r, tt, :], X[0:r, tt, :], ACT.Identity, bias=nbias[0:r, :],
                                     scale=rstd[0:r, :]).then_inc(ln_norm, 1)
            act.wait_ge(top_done, 1)
            for tt in range(NT + 1):
                r = NS if small(tt) else P
                ins = nc.scalar.activation(gat[0:r, tt, :], top8[0:r, tt, 0:TOPK], ACT.Exp, bias=ntop[0:r, tt:tt + 1],
                                           accum_out=gsum[0:r, tt:tt + 1])
            ins.then_inc(gexp_done, 1)
            act.wait_ge(tab_ready, 1)

            act.sem_inc(y_read, 1)

            def expert_block(j):
                for i in range(4):
                    act.wait_ge(g_ready, j * 4 + (i + 1))
                    nc.scalar.activation(sg, gt, ACT.Sigmoid, scale=SWI).then_inc(sig_ready, 1)
                act.wait_ge(chunk_used, j * 12 + 12)
                act.wait_ge(cur_ready, j + 1)
                act.wait_ge(y_out, j * 16 + 16)
                for half in range(2):
                    ins = nc.scalar.mul(ysb[:, 512 * half:512 * half + 512], bank(4 + half), cur[:, 2:3])
                ins.then_inc(y_read, 1)

            with act.Fori(0, E) as j:
                expert_block(j)
            n_over = act.value_load(tabi[0:1, 196:197], min_val=0, max_val=OVER)
            with act.Fori(0, OVER) as q:
                with act.If(q < n_over):
                    expert_block(q + E)
            for tt in range(NT + 1):
                r = NS if small(tt) else P
                act.wait_ge(f_nb, tt + 1)
                nc.scalar.activation(zb[tt % 2][0:r, :], zb[tt % 2][0:r, :], ACT.Identity, bias=nbias[0:r, :],
                                     scale=rstd[0:r, :]).then_inc(f_norm, 1)

        @block.tensor
        def _(pe):
            mm, tr = nc.tensor.matmul, nc.tensor.transpose

            def emptied_unit(*key):
                u = unit_index(*key)
                who = PLAN[u][3]
                pe.wait_ge(unit_act if who == "act" else unit_dve, emptied(u + 1, who))

            pe.wait_ge(cst_in, 16)
            pe.wait_ge(rel_in, 32)
            mm(bank(7)[0:HA, 0:RELW], relt, rel_c[:, 0:RELW], start=True, stop=True).then_inc(rel_mm, 1)
            for u, (kind, a, b, who) in enumerate(PLAN):
                dst = bank(u % BANKS_A)
                if u >= BANKS_A:
                    old = u - BANKS_A
                    pe.wait_ge(unit_act if PLAN[old][3] == "act" else unit_dve, emptied(old + 1, PLAN[old][3]))
                if kind == "x":
                    if b == 0:
                        pe.wait_ge(x_in[a], 32 if small(a) else 16)
                    r = rows_of(a)
                    for k in range(4):
                        ins = tr(dst[:, P * k:P * k + r], X[0:r, a, P * (4 * b + k):P * (4 * b + k) + P], ident[0:r, 0:r])
                elif kind in ("o", "kv", "v"):
                    if b == 0:
                        pe.wait_ge(slot_in[a % STREAM], streamed(a))
                    if a == 0 and b == 0:
                        emptied_unit("x", NT, 0)
                        emptied_unit("x", NT, 1)
                    for k in range(KT):
                        ins = mm(dst[0:rows_of(b), 0:CH], xT[:, k, cols_of(b)], chunk(a % STREAM)[:, k, :],
                                 start=(k == 0), stop=(k == KT - 1))
                elif kind == "g":
                    pe.wait_ge(wg_ready, 1)
                    n = SM if b else SEQ
                    for k in range(KT):
                        ins = mm(dst[0:36, 0:n], wgp[:, k, :], xT[:, k, SEQ * b:SEQ * b + n],
                                 start=(k == 0), stop=(k == KT - 1))
                elif kind in ("k", "q", "a"):
                    c, m = a // 2, a % 2
                    if m == 0 and b == 0:
                        pe.wait_ge(slot_in[c % STREAM], streamed(c))
                    n = SM if b else SEQ
                    for k in range(KT):
                        ins = mm(dst[:, 0:n], chunk(c % STREAM)[:, k, P * m:P * m + P], xT[:, k, SEQ * b:SEQ * b + n],
                                 start=(k == 0), stop=(k == KT - 1))
                elif kind == "gc":
                    pe.wait_ge(gate_rows, 1)
                    for tt in range(NT + 1):
                        ins = tr(dst[0:rows_of(tt), 68 * tt:68 * tt + 68], ST[:, cols_of(tt)], ident[0:68, 0:68])
                elif kind == "ms":
                    for h in range(H):
                        ins = mm(dst[:, SM * h:SM * h + SM], ident[0:H, h:h + 1].to_broadcast([H, P]), ra[:, SEQ:COLS],
                                 start=True, stop=True)
                elif kind == "mb":
                    ins = mm(dst, ident[0:H, a:a + 1].to_broadcast([H, P]), ra[:, 0:SEQ], start=True, stop=True)
                elif kind == "kn":
                    if a == 0:
                        emptied_unit("k", 13, 1)
                        emptied_unit("k", 13, 0)
                        emptied_unit("q", 17, 1)
                        emptied_unit("q", 17, 0)
                    for t in range(NT):
                        ins = tr(dst[:, P * t:P * t + P], kmT[:, a, P * t:P * t + P], ident)
                elif kind == "kns":
                    for h in range(H):
                        ins = tr(dst[0:SM, P * h:P * h + P], kmT[:, h, SEQ:COLS], ident)
                elif kind == "kaT":
                    if a == 0:
                        emptied_unit("kv", 2, NT)
                    for t in range(NT) if a == 0 else [NT]:
                        o = P * t if a == 0 else 0
                        ins = tr(dst[:, o:o + rows_of(t)], kva[0:rows_of(t), t, 0:P], ident[0:rows_of(t), 0:rows_of(t)])
                elif kind == "qs":
                    for h in range(H):
                        ins = tr(dst[0:NS, P * h:P * h + P], qmT[:, h, SEQ:SEQ + NS], ident)
                elif kind == "st":
                    for n in range(NT):
                        ins = mm(dst[:, P * n:P * n + P], kmT[:, a, P * n:P * n + P], qmT[:, a, P * n:P * n + P],
                                 start=True, stop=True)
                ins.then_inc(unit_mm, 1)

            emptied_unit("st", H - 1, 0)
            emptied_unit("kn", H - 1, 0)

            def new_state(n, k_rows, wv):
                pe.wait_ge(wv_ready, n)
                for h in range(H):
                    ins = mm(heads(4)[:, h, :], k_rows[:, DV * h:DV * h + DV], wv[:, h, :], start=True, stop=True)
                ins.then_inc(state_mm, 1)

            new_state(1, kn[0:SM, NT, :], WV[0:SM])
            for n in range(NT):
                pe.wait_ge(state_ready, n + 1)
                if n:
                    pe.wait_ge(chunk_read, n)
                for h in range(H):
                    mm(heads(0)[:, h, :], qmT[:, h, P * n:P * n + P], CT[:, h, :], start=True, stop=True)
                for h in range(H):
                    ins = mm(heads(2)[:, h, :], Pm[:, h, n, :], vaug[:, n, :].rearrange("p (h c) -> p h c", h=H)[:, h, :],
                             start=True, stop=True)
                ins.then_inc(out_mm, 1)
                new_state(n + 2, kn[:, n, :], WV)
            pe.wait_ge(state_ready, NT + 1)
            pe.wait_ge(chunk_read, NT)
            for h in range(H):
                tr(bank(0)[:, DV * h:DV * h + DV], CT[:, h, 0:DV], ident)
            tr(bank(1)[0:H, 0:P], CT[:, :, DV], ident).then_inc(fin_mm, 1)

            pe.wait_ge(s_sel, 1)
            mm(bank(6)[:, 0:NS * H], ones[0:NS, :], Asel.rearrange("p b h -> p (b h)"), start=True, stop=True).then_inc(s_amm, 1)
            pe.wait_ge(fin_copied, 1)
            for b in range(NS):
                if b >= 2:
                    pe.wait_ge(s_num, b - 1)
                pe.wait_ge(s_vm, b + 1)
                for h in range(H):
                    mm(bank(b % 2)[:, DV * h:DV * h + DV], vms[b % 2][:, DV * h:DV * h + DV], kn[0:NS, NT, DV * h:DV * h + DV],
                       start=True, stop=True)
                mm(bank(2 + b % 2), ident[0:NS, b:b + 1].to_broadcast([NS, P]), qs, start=True, stop=True).then_inc(s_outer, 1)
            pe.wait_ge(s_num, NS)
            for h in range(H):
                ins = tr(bank(4)[0:NS, DV * h:DV * h + DV], NUMS[:, :, h], ident)
            ins.then_inc(s_numt, 1)

            pe.wait_ge(ch_in, 16)
            pe.wait_ge(cnew_in, 16 * 2 * NS)
            for b in range(NS):
                ins = tr(bank(b // 4)[:, P * (b % 4):P * (b % 4) + P], cK[:, b, :], ident)
            ins.then_inc(sk_mm, 1)
            pe.wait_ge(sk_cp, 1)
            emptied_unit("a", 21, 1)
            for kv in range(2):
                for b in range(NS):
                    ins = mm(bank(2 + kv)[:, G * b:G * b + G], KTs[HD * kv:HD * kv + HD, b, :],
                             qaS[HD * kv:HD * kv + HD, :, b], start=True, stop=True)
            ins.then_inc(ss_mm, 1)
            pe.wait_ge(ss_cp, 1)
            tr(bank(4)[0:64, 0:P], STs, ident).then_inc(st_mm, 1)
            pe.wait_ge(s_pn, 1)
            tr(bank(5)[:, 0:64], SEx, ident[0:64, 0:64]).then_inc(sp_mm, 1)
            pe.wait_ge(sp_cp, 1)
            pe.wait_ge(cv_in, 16)
            for kv in range(2):
                for b in range(NS):
                    o = 32 * kv + G * b
                    ins = mm(bank(6)[0:HD, o:o + G], cV[:, b, HD * kv:HD * kv + HD], PTs[:, o:o + G], start=True, stop=True)
            ins.then_inc(so_mm, 1)
            pe.wait_ge(so_cp, 1)
            for h in range(HA):
                o = 32 * (h // G) + h % G
                ins = tr(bank(7)[0:NS, HD * h:HD * h + HD], OTs[:, o:o + 29:G], ident[0:HD, 0:HD])
            ins.then_inc(sot_mm, 1)

            emptied_unit("kaT", 0, 0)
            emptied_unit("a", 21, 0)
            pe.wait_ge(s_att, 1)
            for n in range(NT):
                if n:
                    pe.wait_ge(at_out, n)
                for h in range(HA):
                    c, pr = h % G, slice(HD * (h // G), HD * (h // G) + HD)
                    dst = bank(h // 2)[:, 256 * (h % 2):256 * (h % 2) + 256]
                    q = qaT[pr, c, P * n:P * n + P]
                    if n == 0:
                        mm(dst[:, 0:SM], q, kaT[pr, SEQ:COLS], start=True, stop=True)
                        ins = mm(dst[:, P:2 * P], q, kaT[pr, 0:P], start=True, stop=True)
                    else:
                        ins = mm(dst, q, kaT[pr, P * (n - 1):P * (n + 1)], start=True, stop=True)
                    if h % 4 == 3:
                        ins.then_inc(at_mm, 1)
                for h in range(HA):
                    if h % 4 == 0:
                        pe.wait_ge(at_exp, 2 * n + 1 + h // 4)
                    if h % 4 == 0 and n:
                        pe.wait_ge(at_pt, 2 * n - 1 + h // 4)
                    for kb in range(2):
                        i = 2 * h + kb
                        w = SM if n == 0 and kb == 0 else P
                        ins = tr(bank(4 + i // 4)[0:w, P * (i % 4):P * (i % 4) + P], Ssb[:, h, P * kb:P * kb + w], ident)
                    if h % 4 == 3:
                        ins.then_inc(at_tr, 1)
                for h in range(HA):
                    if h % 4 == 0:
                        pe.wait_ge(at_pt, 2 * n + 1 + h // 4)
                    v = slice(P + HD * (h // G), P + HD * (h // G) + HD)
                    k0 = SM if n == 0 else P
                    prev = kva[0:k0, NT if n == 0 else n - 1, v]
                    dst = bank(0)[:, HD * h:HD * h + HD]
                    mm(dst, PTa[0:k0, 2 * h, :], prev, start=True, stop=False)
                    ins = mm(dst, PTa[:, 2 * h + 1, :], kva[:, n, v], start=False, stop=True)
                ins.then_inc(at_pv, 1)

            pe.wait_ge(at_out, NT)
            def project(tt):
                r = NS if small(tt) else P
                pe.wait_ge(rms_scaled, tt + 1)
                if tt >= 2:
                    pe.wait_ge(x1_cp, tt - 1)
                for k in range(KT):
                    ins = tr(bank(k // 4)[:, P * (k % 4):P * (k % 4) + r], mix[0:r, tt, P * k:P * k + P], ident[0:r, 0:r])
                ins.then_inc(mt_mm, 1)
                pe.wait_ge(mt_cp, tt + 1)
                if tt >= 2:
                    pe.wait_ge(ln_stat, tt - 1)
                for half in range(2):
                    for k in range(KT):
                        s = len(CHUNKS) + k // 2
                        if tt == 0 and half == 0 and k % 2 == 0:
                            pe.wait_ge(slot_in[s % STREAM], streamed(s))
                        ins = mm(bank(2 + 2 * (tt % 2) + half)[0:r, :], mixT[tt % 2][:, k, 0:r],
                                 rowpair(s % STREAM)[:, k % 2, 512 * half:512 * half + 512],
                                 start=(k == 0), stop=(k == KT - 1))
                ins.then_inc(op_mm, 1)

            project(0)
            for tt in range(NT + 1):
                r = NS if small(tt) else P
                if tt < NT:
                    project(tt + 1)
                pe.wait_ge(x1_done, tt + 1)
                for k in range(KT):
                    ins = tr(bank(k // 4)[:, P * (k % 4):P * (k % 4) + r], X[0:r, tt, P * k:P * k + P], ident[0:r, 0:r])
                ins.then_inc(x1_mm, 1)
                pe.wait_ge(x1_cp, tt + 1)
                if tt == 0:
                    pe.wait_ge(router_in, 32)
                else:
                    pe.wait_ge(lg_done, tt)
                for k in range(KT):
                    ins = mm(bank(6)[0:r, 0:E], mixT[tt % 2][:, k, 0:r], wr[:, k, :], start=(k == 0), stop=(k == KT - 1))
                ins.then_inc(lg_mm, 1)
            pe.wait_ge(b1_in, 16)
            for c in range(16):
                ins = tr(bank(0)[:, E * c:E * c + E], b1rows[:, 256 * (c // 2) + c % 2:256 * (c // 2) + 255 + c % 2:2],
                         ident[0:E, 0:E])
            ins.then_inc(b1_mm, 1)
            pe.wait_ge(sel_ready, 1)
            for tt in range(NT + 1):
                for t in range(tt):
                    mm(bank(2)[:, E * tt:E * tt + E], ones, SEL[:, t, :], start=(t == 0), stop=False)
                mm(bank(2)[:, E * tt:E * tt + E], strict, SEL[:, tt, :], start=(tt == 0), stop=True)
            for t in range(NT + 1):
                ins = mm(bank(3)[:, 0:E], ones, SEL[:, t, :], start=(t == 0), stop=(t == NT))
            ins.then_inc(rank_mm, 1)

            def list_block(j):
                pe.wait_ge(p_ready, j + 1)
                for t in range(NT + 1):
                    ins = mm(bank(6)[:, 0:3], PS1[:, t, :], v3[:, t, :], start=(t == 0), stop=(t == NT))
                ins.then_inc(idx_mm, 1)

            def turn_block(j):
                pe.wait_ge(xg_in, j * 16 + 16)
                for k in range(KT):
                    ins = tr(bank(2 + k // 4)[:, P * (k % 4):P * (k % 4) + P], xg[:, P * k:P * k + P], ident)
                ins.then_inc(xt_mm, 1)

            def first_product(j):
                for i in range(4):
                    pe.wait_ge(h_read, j * 4 + (i + 1))
                    for c in (2 * i, 2 * i + 1):
                        pe.wait_ge(slot_in[SLOT[c]], moe_landed(c, j))
                        for par in range(2):
                            o = P * (2 * (c % 2) + par)
                            for k in range(KT):
                                ins = mm(bank(i % 2)[:, o:o + P], chunk(SLOT[c])[:, k, par:par + 255:2],
                                         xgT[:, k, :], start=(k == 0), stop=(k == KT - 1))
                        ins.then_inc(chunk_used, 1)
                    if i == 0:
                        pe.wait_ge(idx_ready, j + 1)
                        list_block(j + 1)

            def expert_block(j):
                pe.wait_ge(xt_ready, j + 1)
                first_product(j)
                pe.wait_ge(y_read, j + 1)
                for d in range(4):
                    pe.wait_ge(slot_in[SLOT[8 + d]], moe_landed(8 + d, j))
                    pe.wait_ge(a_ready, j * 4 + (d + 1))
                    for f in (2 * d, 2 * d + 1):
                        for half in range(2):
                            ins = mm(bank(4 + half), aT[:, f, :], rowpair(SLOT[8 + d])[:, f % 2, 512 * half:512 * half + 512],
                                     start=(f == 0), stop=(f == KT - 1))
                    ins.then_inc(chunk_used, 1)
                    if d == 1:
                        turn_block(j + 1)

            list_block(0)
            turn_block(0)
            with pe.Fori(0, E) as j:
                expert_block(j)
            n_over = pe.value_load(tabi[0:1, 196:197], min_val=0, max_val=OVER)
            with pe.Fori(0, OVER) as q:
                with pe.If(q < n_over):
                    expert_block(q + E)
            pe.wait_ge(idx_ready, n_over + (E + 1))
            for tt in range(NT + 1):
                ins = tr(bank(6 + tt // 4)[0:E, P * (tt % 4):P * (tt % 4) + P], GT_[:, tt, :], ident)
            ins.then_inc(gt_mm, 1)
            pe.wait_ge(gt_cp, 1)
            pe.wait_ge(b2_in, 16)
            pe.wait_ge(y_read, n_over + (E + 1))
            for tt in range(NT + 1):
                r = NS if small(tt) else P
                if tt >= 2:
                    pe.wait_ge(b2_read, tt - 1)
                for half in range(2):
                    ins = mm(bank(2 * (tt % 2) + half)[0:r, :], GTT[:, P * tt:P * tt + r], b2sb[:, 512 * half:512 * half + 512],
                             start=True, stop=True)
                ins.then_inc(b2_mm, 1)

        @block.vector
        def _(dve):
            V = nc.vector
            link = Chain(dve, dve_chain)
            V.memset(X[0:64, NT, :], 0.0).then_inc(zeroed, 1)
            V.memset(wgp, 0.0)
            link(V.memset(ST, 0.0))
            vh = vaug[:, :, :].rearrange("p t (h c) -> p t h c", h=H)
            link(V.memset(vh[:, :, :, DV:DV + 1], 1.0))
            dve.wait_ge(wg_in, 16)
            V.tensor_copy(wgp[:, :, 0:4], wgs[:, :, 0:4])
            V.tensor_copy(wgp[:, :, 32:36], wgs[:, :, 4:8]).then_inc(wg_ready, 1)
            dve.wait_ge(rel_mm, 1)
            V.tensor_tensor(relx, bank(7)[0:HA, 0:RELW], rel_c[0:HA, RELW:2 * RELW], ALU.add).then_inc(rel_done, 1)
            dve.wait_ge(gb_in, 16 * (5 + 2 * NS))
            pmeta, pprompt = slice(SEQ + META, COLS), slice(0, SEQ)
            smp = slice(SEQ, SEQ + NS)

            for u, (kind, a, b, who) in enumerate(PLAN):
                if who != "dve":
                    continue
                if kind == "st":
                    dve.wait_ge(exp_intra, a + 1)
                dve.wait_ge(unit_mm, u + 1)
                src = bank(u % BANKS_A)
                if kind == "x":
                    r = rows_of(a)
                    ins = V.tensor_copy(xT[:, 4 * b:4 * b + 4, cols_of(a)],
                                        src.rearrange("p (k n) -> p k n", n=P)[:, :, 0:r])
                elif kind == "kv":
                    ins = V.tensor_copy(kva[0:rows_of(b), b, :], src[0:rows_of(b), 0:CH])
                elif kind == "v":
                    r = rows_of(b)
                    h0 = 2 * (a - 3)
                    ins = V.tensor_copy(vh[0:r, b, h0:h0 + 2, 0:DV], src[0:r, 0:CH].rearrange("p (h c) -> p h c", h=2))
                elif kind == "g":
                    cs = slice(SEQ, COLS) if b else pprompt
                    n = SM if b else SEQ
                    link(V.tensor_scalar(ra[:, cs], src[0:4, 0:n], big_b[0:4, :], None, ALU.add))
                    ins = V.tensor_scalar(rb[:, cs], src[32:36, 0:n], bf_b[32:36, :], None, ALU.add)
                elif kind == "k":
                    ins = V.tensor_scalar(kmT[:, a - 10, SEQ:COLS], src[:, 0:SM], float(DV) ** -0.5, None, ALU.mult)
                elif kind == "q":
                    ins = V.tensor_copy(qmT[:, a - 14, SEQ:COLS], src[:, 0:SM])
                elif kind == "a":
                    ins = V.tensor_copy(qaS[:, a - 18, :], src[:, 0:NS])
                elif kind == "gc":
                    g = src[:, 0:68 * (NT + 1)].rearrange("p (t c) -> p t c", c=68)
                    link(V.tensor_copy(GC[:, 0:NT, :], g[:, 0:NT, :]))
                    ins = V.tensor_copy(GC[0:SM, NT, :], g[0:SM, NT, :])
                elif kind == "ms":
                    ins = V.tensor_copy(Me[:, 0, :], src[:, SM - 1:SM * H:SM])
                elif kind == "mb":
                    link(V.tensor_copy(Me[:, 1:NT + 1, a], src[:, P - 1:SEQ:P]))
                    ins = V.tensor_tensor(Pm[:, a], causal.unsqueeze(1).to_broadcast([P, NT, P]),
                                          src.rearrange("p (n t) -> p n t", n=NT), ALU.subtract)
                elif kind == "kns":
                    dve.wait_ge(relw_out, 16)
                    ins = V.tensor_copy(kn[0:SM, NT, :], src[0:SM, :])
                elif kind == "kaT":
                    ins = V.tensor_copy(kaT[:, SEQ:COLS], src[:, 0:SM])
                elif kind == "qs":
                    ins = V.tensor_copy(qs, src[0:NS, :])
                elif kind == "st":
                    ins = V.tensor_tensor(Pm[:, a], Pm[:, a], src.rearrange("p (n t) -> p n t", n=NT), ALU.mult)
                ins.then_inc(unit_dve, 1)
                dve.wait_ge(unit_dve, emptied(u + 1, "dve"))
                if (kind, b) == ("g", 1):
                    V.scalar_tensor_tensor(rc, rb, -1.0, rb, ALU.mult, ALU.max).then_inc(gate_abs, 1)
                if (kind, a, b) == ("v", 4, NT):
                    dve.wait_ge(gate_ln, 1)
                    link(V.scalar_tensor_tensor(rb, rb, 0.0, rc, ALU.min, ALU.subtract))
                    link(V.tensor_copy(ST[32:36, smp], rb[:, smp]))
                    link(V.tensor_copy(ST[0:4, smp], ra[:, smp]))
                    one = ones[0:4, 0:1]
                    for dst, data, op in ((rc, rb, ALU.add), (ra, rb, ALU.max)):
                        for cs, n, init in ((pmeta, NM, 0.0), (pprompt, SEQ, dst[:, COLS - 1:COLS])):
                            link(V.tensor_tensor_scan(dst[:, cs], one.to_broadcast([4, n]), data[:, cs], init, ALU.mult, op))
                        if dst is rc:
                            for cs in (pmeta, pprompt):
                                link(V.tensor_tensor(rb[:, cs], ra[:, cs], rc[:, cs], ALU.subtract))
                    for cs in (pmeta, pprompt):
                        link(V.tensor_tensor(ST[64:68, cs], rc[:, cs], ra[:, cs], ALU.add))
                        link(V.tensor_copy(ST[0:4, cs], rb[:, cs]))
                        ins = V.tensor_copy(ST[32:36, cs], ra[:, cs])
                        link(ins) if cs is pmeta else ins.then_inc(gate_rows, 1)
                if (kind, a) == ("mb", H - 1):
                    link(V.tensor_tensor(wg[:, 0:NT, :], GC[:, 0:NT, 0:4], Me[:, 1:NT + 1, :], ALU.subtract))
                    link(V.tensor_tensor(wg[META:SM, NT, :], GC[META:SM, NT, 0:4], Me[META:SM, 0, :], ALU.subtract))
                    link(V.tensor_tensor(dec, Me[:, 0:NT, :], Me[:, 1:NT + 1, :], ALU.subtract))
                    link(V.tensor_tensor(wint, Me[:, 0:NT, :], GC[:, 0:NT, 32:36], ALU.subtract))
                    V.tensor_scalar(emt, GC[:, 0:NT, 64:68], -1.0, None, ALU.mult).then_inc(col_gates, 1)

            def cols4(ap, r0=0, r1=P, n=DV + 1):
                return ap.unsqueeze(2).to_broadcast([r1 - r0, H, n])

            dve.wait_ge(exp_gates, 1)
            link(V.memset(WV[0:64], 0.0))
            link(V.tensor_tensor(WV[META:SM], vh[META:SM, NT], cols4(wg[META:SM, NT, :], META, SM), ALU.mult), wv_ready)
            dve.wait_ge(state_mm, 1)
            link(V.tensor_copy(CT, heads(4)), state_ready)
            for n in range(NT):
                link(V.tensor_tensor(WV, vh[:, n], cols4(wg[:, n, :]), ALU.mult), wv_ready)
                dve.wait_ge(out_mm, n + 1)
                link(V.tensor_tensor(NUM, heads(0), cols4(wint[:, n, :]), ALU.mult))
                link(V.tensor_tensor(NUM, NUM, heads(2), ALU.add), chunk_read)
                dve.wait_ge(state_mm, n + 2)
                link(V.tensor_tensor(CT, CT, cols4(dec[:, n, :]), ALU.mult))
                link(V.tensor_tensor(CT, CT, heads(4), ALU.add), state_ready)
                d4 = den4[:, 0:4]
                link(V.scalar_tensor_tensor(d4, NUM[:, :, DV], -1.0, NUM[:, :, DV], ALU.mult, ALU.max))
                link(V.tensor_tensor(d4, d4, emt[:, n, :], ALU.max))
                link(V.reciprocal(d4, d4))
                mh = mix[:, n, 0:512].rearrange("p (h c) -> p h c", h=H)
                link(V.tensor_tensor(mh, mh, NUM[:, :, 0:DV], ALU.mult))
                link(V.tensor_tensor(mh, mh, cols4(d4, n=DV), ALU.mult))
            dve.wait_ge(fin_mm, 1)
            link(V.tensor_copy(WV.rearrange("p h c -> p (h c)")[:, 0:512], bank(0)))
            link(V.tensor_copy(nfin, bank(1)[0:H, 0:P]), fin_copied)

            dve.wait_ge(sm_in, 16)
            dve.wait_ge(sn_in, 16)
            dve.wait_ge(sc_in, 16)
            ig, lf = GC[0:NS, NT, 0:4], GC[0:NS, NT, 32:36]
            link(V.tensor_tensor(sd, lf, sm_st, ALU.add))
            link(V.tensor_tensor(smt, sd, ig, ALU.max))
            link(V.tensor_tensor(sa, sd, smt, ALU.subtract))
            link(V.tensor_tensor(sw, ig, smt, ALU.subtract), s_gates)
            dve.wait_ge(s_exp, 1)
            link(V.tensor_tensor(Asel, ident[0:NS, 0:NS].unsqueeze(2).to_broadcast([NS, NS, H]),
                                 sa.unsqueeze(1).to_broadcast([NS, NS, H]), ALU.mult), s_sel)

            def h8(ap):
                return ap.rearrange("p (h c) -> p h c", h=H)

            kns_ = h8(kn[0:NS, NT, :])
            link(V.tensor_tensor(kns_, kns_, cols4(sw, 0, NS, DV), ALU.mult))
            link(V.tensor_tensor(h8(nsb), h8(nsb), cols4(sa, 0, NS, DV), ALU.mult))
            link(V.tensor_tensor(nsb, nsb, kn[0:NS, NT, :], ALU.add))
            link(V.tensor_tensor(vm, nsb, qs, ALU.mult))
            link(V.tensor_reduce(sden, h8(vm), AX, ALU.add))
            link(V.scalar_tensor_tensor(sden, sden, -1.0, sden, ALU.mult, ALU.max))
            link(V.tensor_tensor(sden, sden, s_em, ALU.max))
            link(V.reciprocal(sden, sden))
            dve.wait_ge(s_amm, 1)
            link(V.tensor_copy(abc.rearrange("p b h -> p (b h)"), bank(6)[:, 0:NS * H]), s_abc)
            tmp = NUM.rearrange("p h c -> p (h c)")[:, 0:512].rearrange("p (h c) -> p h c", h=H)

            def own_value(b):
                link(V.tensor_scalar(h8(vms[b % 2]), vh[0:NS, NT, :, 0:DV], ident[0:NS, b:b + 1], None, ALU.mult), s_vm)

            own_value(0)
            for b in range(NS):
                if b + 1 < NS:
                    own_value(b + 1)
                Cb = Cst[:, H * b:H * b + H, :]
                dve.wait_ge(s_scaled, b + 1)
                dve.wait_ge(s_outer, b + 1)
                link(V.tensor_tensor(Cb, Cb, h8(bank(b % 2)), ALU.add))
                link(V.tensor_tensor(tmp, Cb, h8(bank(2 + b % 2)), ALU.mult))
                link(V.tensor_reduce(NUMS[:, b, :], tmp, AX, ALU.add), s_num)
            dve.wait_ge(s_numt, 1)
            msr = h8(mix[0:NS, NT, 0:512])
            link(V.tensor_tensor(msr, msr, h8(bank(4)[0:NS, :]), ALU.mult))
            link(V.tensor_tensor(msr, msr, cols4(sden, 0, NS, DV), ALU.mult), s_hdone)

            dve.wait_ge(ss_mm, 1)
            link(V.tensor_scalar(STs[:, 0:32], bank(2)[:, 0:32], HD ** -0.5, None, ALU.mult))
            link(V.tensor_scalar(STs[:, 32:64], bank(3)[:, 0:32], HD ** -0.5, None, ALU.mult), ss_cp)
            dve.wait_ge(st_mm, 1)
            dve.wait_ge(bs_in, 16 * 2 * NS)
            link(V.tensor_tensor(SEx, bank(4)[0:64, 0:P], bSs, ALU.add))
            link(V.tensor_reduce(sks[:, 1:2], SEx, AX, ALU.max))
            link(V.tensor_tensor(sks[:, 1:2], sks[:, 1:2], sks[:, 0:1], ALU.max))
            link(V.tensor_scalar(sks[:, 1:2], sks[:, 1:2], -1.0, None, ALU.mult), s_max)
            dve.wait_ge(s_aexp, 1)
            link(V.tensor_tensor(sks[:, 2:3], sks[:, 2:3], sks[:, 3:4], ALU.add))
            link(V.reciprocal(sks[:, 2:3], sks[:, 2:3]))
            link(V.tensor_scalar(SEx, SEx, sks[:, 2:3], None, ALU.mult), s_pn)
            dve.wait_ge(sp_mm, 1)
            link(V.tensor_copy(PTs, bank(5)[:, 0:64]), sp_cp)
            dve.wait_ge(so_mm, 1)
            link(V.tensor_copy(OTs, bank(6)[0:HD, 0:64]), so_cp)
            dve.wait_ge(sot_mm, 1)
            dve.wait_ge(ns_done, 16)
            dve.wait_ge(prompt_C_out, 32)
            link(V.tensor_copy(mix[0:NS, NT, 512:1024], bank(7)[0:NS, :]), s_att)

            dve.wait_ge(band_in, 16)
            S4 = PS[:, 0:4, :].rearrange("p b (h k) -> p (b h) k", h=2)
            for n in range(NT):
                for half in range(2):
                    hs = slice(4 * half, 4 * half + 4)
                    Sh, Bh, Qh = Ssb[:, hs], band[:, hs], S4[:, hs]
                    if n:
                        dve.wait_ge(at_tr, 2 * n - 1 + half)
                    dve.wait_ge(at_mm, 2 * n + half + 1)
                    if n == 0:
                        link(V.memset(Sh[:, :, 0:P], NEG))
                        link(V.scalar_tensor_tensor(Sh[:, :, META:SM], Qh[:, :, META:SM], HD ** -0.5, Bh[:, :, P - NM:P],
                                                    ALU.mult, ALU.add))
                        link(V.scalar_tensor_tensor(Sh[:, :, P:2 * P], Qh[:, :, P:2 * P], HD ** -0.5, Bh[:, :, P:2 * P],
                                                    ALU.mult, ALU.add))
                    else:
                        link(V.scalar_tensor_tensor(Sh, Qh, HD ** -0.5, Bh, ALU.mult, ALU.add))
                    link(V.tensor_reduce(mx8[:, hs], Sh, AX, ALU.max))
                    link(V.tensor_tensor(mx8[:, hs], mx8[:, hs], sinkb[:, hs], ALU.max))
                    link(V.tensor_scalar(nmx8[:, hs], mx8[:, hs], -1.0, None, ALU.mult))
                    link(V.tensor_tensor(esk[:, hs], sinkb[:, hs], mx8[:, hs], ALU.subtract), at_max)
                dve.wait_ge(at_exp, 2 * n + 2)
                link(V.tensor_tensor(den4, sum8, esk, ALU.add))
                link(V.reciprocal(den4, den4))
                dve.wait_ge(at_pv, n + 1)
                link(V.tensor_tensor(mix[:, n, 512:1024].rearrange("p (h c) -> p h c", h=HA),
                                     bank(0).rearrange("p (h c) -> p h c", h=HA),
                                     den4.unsqueeze(2).to_broadcast([P, HA, HD]), ALU.mult), at_out)

            dve.wait_ge(ln_in, 32)
            dve.wait_ge(router_in, 32)
            def turned_rows(tt):
                r = NS if small(tt) else P
                dve.wait_ge(mt_mm, tt + 1)
                link(V.tensor_tensor(mixT[tt % 2][:, :, 0:r], PS[:, 0:2, :].rearrange("p b (k n) -> p (b k) n", n=P)[:, :, 0:r],
                                     gcol.unsqueeze(2).to_broadcast([P, KT, r]), ALU.mult), mt_cp)

            turned_rows(0)
            for tt in range(NT + 1):
                r = NS if small(tt) else P
                if tt < NT:
                    turned_rows(tt + 1)
                mT = mixT[tt % 2]
                dve.wait_ge(op_mm, tt + 1)
                z = X[0:r, tt, :]
                b0 = 2 + 2 * (tt % 2)
                link(V.scalar_tensor_tensor(z, z, ALPHA, PS[0:r, b0:b0 + 2, :].rearrange("p b n -> p (b n)"), ALU.mult, ALU.add))
                for half in range(2):
                    link(V.bn_stats(bst[0:r, 6 * half:6 * half + 6], z[:, 512 * half:512 * half + 512]))
                link(V.bn_aggr(bag[0:r, 0:2], bst[0:r, :]), ln_stat)
                dve.wait_ge(ln_pow, tt + 1)
                link(V.scalar_tensor_tensor(nbias[0:r], bag[0:r, 0:1], -1.0, rstd[0:r], ALU.mult, ALU.mult), ln_nb)
                dve.wait_ge(ln_norm, tt + 1)
                link(V.tensor_tensor(z, z, lng[0:r, :], ALU.mult))
                link(V.tensor_tensor(z, z, lnb[0:r, :], ALU.add), x1_done)
                dve.wait_ge(x1_mm, tt + 1)
                link(V.tensor_copy(mT[:, :, 0:r], PS[:, 0:2, :].rearrange("p b (k n) -> p (b k) n", n=P)[:, :, 0:r]), x1_cp)
                dve.wait_ge(lg_mm, tt + 1)
                link(V.tensor_tensor(LG[0:r, tt, :], bank(6)[0:r, 0:E], br[0:r, :], ALU.add), lg_done)
            dve.wait_ge(b1_mm, 1)
            link(V.tensor_copy(b1T.rearrange("p c e -> p (c e)"), bank(0)), b1_cp)

            dve.wait_ge(iota_done, 1)
            link(V.memset(idxf, 99.0))
            link(V.memset(gat, 0.0))
            link(V.memset(gsum, 1.0))
            for tt in range(NT + 1):
                r = NS if small(tt) else P
                link(V.max(top8[0:r, tt, :], LG[0:r, tt, :]))
                link(V.max_index(idx8[0:r, tt, :].bitcast(U32), top8[0:r, tt, :], LG[0:r, tt, :]))
                link(V.tensor_copy(idxf[0:r, tt, :], idx8[0:r, tt, 0:TOPK].bitcast(U32)))
                link(V.tensor_scalar(ntop[0:r, tt:tt + 1], top8[0:r, tt, 0:1], -1.0, None, ALU.mult),
                     top_done if small(tt) else None)
            dve.wait_ge(gexp_done, 1)
            link(V.reciprocal(gsum, gsum))
            link(V.tensor_tensor(gat, gat, gsum.unsqueeze(2).to_broadcast([P, NT + 1, TOPK]), ALU.mult))
            n20 = (NT + 1) * TOPK
            OHf = OH.rearrange("p t k e -> p (t k) e")
            OGf = OG.rearrange("p t k e -> p (t k) e")
            link(V.tensor_tensor(OHf, iota[:, 0:E].unsqueeze(1).to_broadcast([P, n20, E]),
                                 idxf.rearrange("p t k -> p (t k)").unsqueeze(2).to_broadcast([P, n20, E]), ALU.is_equal))
            link(V.tensor_reduce(SEL, OH.rearrange("p t k e -> p t e k"), AX, ALU.add), sel_ready)
            link(V.tensor_tensor(OGf, OHf, gat.rearrange("p t k -> p (t k)").unsqueeze(2).to_broadcast([P, n20, E]), ALU.mult))
            link(V.tensor_reduce(GT_, OG.rearrange("p t k e -> p t e k"), AX, ALU.add))
            link(V.tensor_copy(T2[:, :, :, 1], GT_))
            for k in range(TOPK):
                link(V.tensor_scalar(OG[:, :, k, :], OH[:, :, k, :], float(k), None, ALU.mult))
            link(V.tensor_reduce(T2[:, :, :, 0], OG.rearrange("p t k e -> p t e k"), AX, ALU.add))
            link(V.tensor_scalar(tok4, tokid, float(TOPK), -BIG, ALU.mult, ALU.add))
            link(V.tensor_tensor(T2[:, :, :, 0], T2[:, :, :, 0], tok4.unsqueeze(2).to_broadcast([P, NT + 1, E]), ALU.add))
            link(V.tensor_copy(v3[:, :, 0], tokid))
            dve.wait_ge(rank_mm, 1)
            link(V.scalar_tensor_tensor(RK.rearrange("p t e -> p (t e)"), bank(2)[:, 0:160], 1.0,
                                        SEL.rearrange("p t e -> p (t e)"), ALU.add, ALU.mult))
            link(V.tensor_scalar(RK, RK, -1.0, None, ALU.add))
            link(V.tensor_copy(cntf, bank(3)[:, 0:E]))
            cnt = cntf[0:1, :]
            c4 = cmpo[:, 0:4, :].rearrange("p q e -> p (q e)").rearrange("p (e b) -> p e b", b=4)
            link(V.tensor_tensor(c4, cnt.unsqueeze(2).to_broadcast([1, E, 4]),
                                 iota[0:1, P:5 * P:P].unsqueeze(1).to_broadcast([1, E, 4]), ALU.is_gt))
            link(V.tensor_reduce(ovf, c4, AX, ALU.add))
            link(V.tensor_tensor_scan(cum, ones[0:1, 0:1].to_broadcast([1, E]), ovf, 0.0, ALU.mult, ALU.add))
            link(V.tensor_tensor(cmpq, cum.unsqueeze(1).to_broadcast([1, OVER, E]),
                                 iota[0:1, 0:OVER].unsqueeze(2).to_broadcast([1, OVER, E]), ALU.is_le))
            link(V.tensor_tensor(cmpo, cmpq, ovf.unsqueeze(1).to_broadcast([1, OVER, E]), ALU.mult))
            link(V.memset(tabf, 0.0))
            link(V.memset(tabf[:, 48, 1:2], 640.0))
            link(V.tensor_copy(tabf[:, 0:E, 0], iota[0:1, 0:E]))
            link(V.tensor_copy(tabf[:, 0:E, 2], cnt))
            to, tb = tabf[:, E:E + OVER, 0], tabf[:, E:E + OVER, 1]
            link(V.tensor_reduce(to, cmpq, AX, ALU.add))
            link(V.tensor_scalar(to, to, float(E - 1), None, ALU.min))
            link(V.tensor_reduce(tb, cmpo, AX, ALU.add))
            link(V.tensor_tensor(tb, iota[0:1, 0:OVER], tb, ALU.subtract))
            link(V.tensor_scalar(tb, tb, 1.0, 5.0, ALU.add, ALU.min))
            link(V.tensor_scalar(tb, tb, float(P), None, ALU.mult))
            link(V.tensor_copy(tab.rearrange("p j c -> p (j c)"), tabf.rearrange("p j c -> p (j c)")))
            link(V.tensor_copy(tabi[0:1, 196:197], cum[:, E - 1:E]), tab_ready)
            link(V.memset(PS[:, 0, :], 0.0), h_read)
            link(V.memset(PS[:, 1, :], 0.0), h_read)

            def list_block(j, e, off):
                link(V.tensor_tensor(PS1, iota[:, bass.ds(off, P)].unsqueeze(1).to_broadcast([P, NT + 1, P]),
                                     RK[:, :, bass.ds(e, 1)].to_broadcast([P, NT + 1, P]), ALU.is_equal))
                link(V.tensor_copy(v3[:, :, 1:3], T2[:, :, bass.ds(e, 1), :].rearrange("p t o c -> p t (o c)")), p_ready)

            def read_list(j):
                dve.wait_ge(idx_mm, j + 1)
                link(V.tensor_copy(nxi[:, 0:1], bank(6)[:, 0:1]))
                link(V.tensor_scalar(nxi[:, 1:2], bank(6)[:, 1:2], BIG, None, ALU.add))
                link(V.tensor_copy(nxt[:, 2:3], bank(6)[:, 2:3]), idx_ready)

            def read_turned(j):
                dve.wait_ge(xt_mm, j + 1)
                link(V.tensor_copy(xgT, PS[:, 2:4, :].rearrange("p b (k n) -> p (b k) n", n=P)), xt_ready, wait=False)

            list_block(0, 0, 0)
            read_list(0)
            read_turned(0)

            def expert_block(j, e):
                link.start_round(j)
                dve.wait_ge(xt_ready, j + 1)
                link(V.tensor_copy(b1c, b1T[:, :, bass.ds(e, 1)].rearrange("p c o -> p (c o)")))
                en = dve.value_load(tab[0:1, bass.ds(j + 1, 1), 0], min_val=0, max_val=E - 1)
                off = dve.value_load(tab[0:1, bass.ds(j + 1, 1), 1], min_val=0, max_val=5 * P)
                list_block(j + 1, en, off)
                for i in range(4):
                    dve.wait_ge(chunk_used, j * 12 + (2 * i + 2))
                    link(V.tensor_tensor(ht, bank(i % 2).rearrange("p (c n) -> p c n", c=4),
                                         b1c[:, 4 * i:4 * i + 4].unsqueeze(2).to_broadcast([P, 4, P]), ALU.add), h_read)
                    link(V.tensor_scalar(gt, ht[:, 0::2, :], LIMIT, None, ALU.min), g_ready)
                    link(V.tensor_scalar(lt, ht[:, 1::2, :], LIMIT, -LIMIT, ALU.min, ALU.max))
                    link(V.scalar_tensor_tensor(lt, lt, 1.0, gt, ALU.add, ALU.mult))
                    dve.wait_ge(sig_ready, j * 4 + (i + 1))
                    link(V.tensor_tensor(aT[:, 2 * i:2 * i + 2, :], lt, sg, ALU.mult), a_ready)
                    if i == 1:
                        dve.wait_ge(y_read, j + 1)
                        dve.wait_ge(y_out, j * 16 + 16)
                        link(V.tensor_copy(cur[:, 0:3], nxt[:, 0:3]), cur_ready)
                        dve.wait_ge(xg_in, j * 16 + 16)
                        read_list(j + 1)
                read_turned(j + 1)
                link.end_round()

            link.loop([(dve_chain, 12), (p_ready, 1), (idx_ready, 1), (xt_ready, 1), (h_read, 4), (g_ready, 4), (a_ready, 4),
                       (cur_ready, 1)])
            with dve.Fori(0, E) as j:
                expert_block(j, j)
            n_over = dve.value_load(tabi[0:1, 196:197], min_val=0, max_val=OVER)
            with dve.Fori(0, OVER) as q:
                with dve.If(q < n_over):
                    e = dve.value_load(tab[0:1, bass.ds(q + E, 1), 0], min_val=0, max_val=E - 1)
                    expert_block(q + E, e)
            link = Chain(dve, f_chain)
            dve.wait_ge(gt_mm, 1)
            link(V.tensor_copy(GTT[:, 0:SEQ], bank(6)[0:E, :]))
            link(V.tensor_copy(GTT[:, SEQ:NTOK], bank(7)[0:E, 0:NS]), gt_cp)
            dve.wait_ge(ln2_in, 32)

            def summed(tt):
                r = NS if small(tt) else P
                Y, z = Yt[tt % 2], zb[tt % 2][0:r, :]
                if tt >= 2:
                    dve.wait_ge(fin_out[tt % 2], 16 * (tt // 2))
                dve.wait_ge(b2_mm, tt + 1)
                b0 = 2 * (tt % 2)
                link(V.scalar_tensor_tensor(z, X[0:r, tt, :], ALPHA, PS[0:r, b0:b0 + 2, :].rearrange("p b n -> p (b n)"),
                                            ALU.mult, ALU.add), b2_read)
                dve.wait_ge(y_half, tt + 1)
                link(V.tensor_tensor(z, z, Y[0:r, 0, :], ALU.add))
                link(V.tensor_tensor(z, z, Y[0:r, 2, :], ALU.add), yt_used)

            summed(0)
            for tt in range(NT + 1):
                r = NS if small(tt) else P
                z = zb[tt % 2][0:r, :]
                for half in range(2):
                    link(V.bn_stats(bst[0:r, 6 * half:6 * half + 6], z[:, 512 * half:512 * half + 512]))
                link(V.bn_aggr(bag[0:r, 0:2], bst[0:r, :]), f_stat)
                dve.wait_ge(f_pow, tt + 1)
                link(V.scalar_tensor_tensor(nbias[0:r], bag[0:r, 0:1], -1.0, rstd[0:r], ALU.mult, ALU.mult), f_nb)
                if tt < NT:
                    summed(tt + 1)
                dve.wait_ge(f_norm, tt + 1)
                link(V.tensor_tensor(z, z, lng[0:r, :], ALU.mult))
                link(V.tensor_tensor(z, z, lnb[0:r, :], ALU.add), f_done)


def constants():
    i = np.arange(P)
    c = np.concatenate([np.eye(P), i[:, None] < i[None, :], np.where(i[:, None] <= i[None, :], 0.0, NEG), np.ones((P, P))],
                       axis=1).astype(np.float32)
    dist = 2 * P - 1 - np.arange(RELW)
    ok = (dist >= 0) & (dist < P)
    d = np.clip(dist, 0, P - 1)
    half = E // 2
    log_b = half + (np.log(np.maximum(d, 1).astype(np.float32) / np.float32(half)) / np.float32(np.log(P / half))
                    * np.float32(E - half)).astype(np.int32)
    bucket = np.where(d < half, d, np.minimum(log_b, E - 1))
    rel = np.zeros((E, 2 * RELW), np.float32)
    rel[:, 0:RELW] = (bucket[None, :] == np.arange(E)[:, None]) & ok[None, :]
    rel[:, RELW:] = np.where(ok, 0.0, NEG)[None, :]
    return c, rel


_INS = ["x_prompt", "x_sample", "cache_swa_k", "cache_swa_v", "state_mlstm_C", "state_mlstm_n", "state_mlstm_m",
        "meta_tokens", "rel_bias", "w_in", "b_igate", "b_fgate", "attn_sinks", "g_mlstm_out", "g_attn_out", "w_out",
        "ln1_g", "ln1_b", "w_router", "b_router", "w_moe1", "b_moe1", "w_moe2", "b_moe2", "ln2_g", "ln2_b"]
_OUTS = [(1, SEQ, D), (NS, 1, D), (1, 1, P, 2, HD), (1, 1, P, 2, HD), (1, 1, H, DV, DV), (1, 1, H, DV), (1, 1, H),
         (1, NS, P, 2, HD), (1, NS, P, 2, HD), (1, NS, H, DV, DV), (1, NS, H, DV), (1, NS, H)]


def kernel(**inputs):
    import numpy as _np
    import concourse.bacc as _bacc
    from concourse import mybir as _mybir
    from concourse.bass_utils import run_bass_kernel_spmd as _run

    nc = _bacc.Bacc("TRN2", target_bir_lowering=False, num_devices=1)
    arrays, args = {}, []
    named = [(n, _np.ascontiguousarray(inputs[n])) for n in _INS] + list(zip(("consts", "rel_consts"), constants()))
    for name, a in named:
        arrays[f"in_{name}_dram"] = a
        args.append(nc.dram_tensor(f"in_{name}_dram", a.shape, _mybir.dt.from_np(a.dtype), kind="ExternalInput").ap())
    for i, shape in enumerate(_OUTS):
        args.append(nc.dram_tensor(f"out_{i}_dram", shape, F32, kind="ExternalOutput").ap())
    decoder_layer(nc, *args)
    r = _run(nc, [arrays], core_ids=[0])
    return tuple(r.results[0][f"out_{i}_dram"] for i in range(len(_OUTS)))
```
